# Optimizing a Trainium2 kernel written in Bass

```python
import jax, jax.numpy as jnp
from jax import lax
import numpy as np
import math

D_MODEL = 2048
BATCH = 1
SEQ = 256
DEPTH = 1

CHUNK = 64
Q_BLOCK = 128
ROPE_THETA = 500000.0
EPS = 1e-6
NEG_INF = -1e30
N_BRANCHES = 2

MLA_HEADS = 8
MLA_NOPE = 128
MLA_ROPE = 64
MLA_V = 128
MLA_Q_RANK = 512
MLA_KV_RANK = 256

DSA_HEADS = 8
DSA_KV_HEADS = 2
DSA_GROUP = DSA_HEADS // DSA_KV_HEADS
DSA_HEAD_DIM = 128
DSA_ROT = DSA_HEAD_DIM // 4
IDX_HEADS = 16
IDX_DIM = 64
IDX_ROT = IDX_DIM // 4
DSA_TOPK_MAX = 256

PEER_HEADS = 8
PEER_N_KEYS = 128
PEER_N_EXPERTS = PEER_N_KEYS * PEER_N_KEYS
PEER_KEY_DIM = 128
PEER_TOPK = 16
PEER_TOKEN_BLOCK = 128

IN_SIZES = (
    MLA_Q_RANK,
    MLA_KV_RANK,
    MLA_ROPE,
    DSA_HEADS * DSA_HEAD_DIM,
    DSA_KV_HEADS * DSA_HEAD_DIM,
    DSA_KV_HEADS * DSA_HEAD_DIM,
    IDX_HEADS * IDX_DIM,
    IDX_DIM,
    IDX_HEADS,
    N_BRANCHES * D_MODEL,
)
IN_WIDTH = sum(IN_SIZES)


def rmsnorm(t, g):
    tf = t.astype(jnp.float32)
    y = tf * lax.rsqrt(jnp.mean(tf * tf, axis=-1, keepdims=True) + EPS)
    return (y * g.astype(jnp.float32)).astype(t.dtype)

def rope(t, positions, rot_dim):
    half = rot_dim // 2
    inv_freq = ROPE_THETA ** (-(jnp.arange(half, dtype=jnp.float32) * 2.0) / rot_dim)
    ang = positions.astype(jnp.float32)[..., None] * inv_freq
    cos = jnp.cos(ang)[:, :, None, :]
    sin = jnp.sin(ang)[:, :, None, :]
    t1 = t[..., :half].astype(jnp.float32)
    t2 = t[..., half:rot_dim].astype(jnp.float32)
    rest = t[..., rot_dim:]
    return jnp.concatenate([(t1 * cos - t2 * sin).astype(t.dtype),
                            (t2 * cos + t1 * sin).astype(t.dtype), rest], axis=-1)

def to_blocks(t):
    B, S = t.shape[:2]
    return t.reshape((B, S // Q_BLOCK, Q_BLOCK) + t.shape[2:]).swapaxes(0, 1)

def from_blocks(t):
    nb, B, qb, w = t.shape
    return t.swapaxes(0, 1).reshape(B, nb * qb, w)

def chunk_causal_attention(q, k, v, scale):
    S = q.shape[1]
    n_blocks = S // Q_BLOCK
    starts = jnp.arange(n_blocks, dtype=jnp.int32) * Q_BLOCK
    key_chunk = jnp.arange(S, dtype=jnp.int32) // CHUNK

    def one_block(args):
        q_blk, q0 = args
        q_chunk = (q0 + jnp.arange(Q_BLOCK, dtype=jnp.int32)) // CHUNK
        allowed = key_chunk[None, :] <= q_chunk[:, None]
        s = jnp.einsum('bqhd,bkhd->bhqk', q_blk, k).astype(jnp.float32) * scale
        s = jnp.where(allowed[None, None], s, NEG_INF)
        p = jax.nn.softmax(s, axis=-1).astype(v.dtype)
        o = jnp.einsum('bhqk,bkhd->bqhd', p, v)
        return o.reshape(o.shape[0], Q_BLOCK, -1)

    return from_blocks(lax.map(one_block, (to_blocks(q), starts)))

def mla_branch(c_q, c_kv, k_rope, positions, q_norm_g, kv_norm_g, w_uq, w_uk, w_uv):
    B, S, _ = c_q.shape
    q = jnp.einsum('bsr,rhd->bshd', rmsnorm(c_q, q_norm_g), w_uq)
    q = jnp.concatenate([q[..., :MLA_NOPE], rope(q[..., MLA_NOPE:], positions, MLA_ROPE)], axis=-1)
    ckv = rmsnorm(c_kv, kv_norm_g)
    k_nope = jnp.einsum('bsr,rhd->bshd', ckv, w_uk)
    v = jnp.einsum('bsr,rhd->bshd', ckv, w_uv)
    k_pe = rope(k_rope[:, :, None, :], positions, MLA_ROPE)
    k = jnp.concatenate([k_nope, jnp.broadcast_to(k_pe, (B, S, MLA_HEADS, MLA_ROPE))], axis=-1)
    return chunk_causal_attention(q, k, v, (MLA_NOPE + MLA_ROPE) ** -0.5)

def dsa_branch(q, k, v, q_idx, k_idx, w_idx, positions):
    B, S, _ = q.shape
    q = rope(q.reshape(B, S, DSA_HEADS, DSA_HEAD_DIM), positions, DSA_ROT)
    k = rope(k.reshape(B, S, DSA_KV_HEADS, DSA_HEAD_DIM), positions, DSA_ROT)
    v = v.reshape(B, S, DSA_KV_HEADS, DSA_HEAD_DIM)
    q_idx = rope(q_idx.reshape(B, S, IDX_HEADS, IDX_DIM), positions, IDX_ROT)
    k_idx = rope(k_idx[:, :, None, :], positions, IDX_ROT)[:, :, 0, :]
    top_k = min(DSA_TOPK_MAX, S // 4)
    n_blocks = S // Q_BLOCK
    starts = jnp.arange(n_blocks, dtype=jnp.int32) * Q_BLOCK
    key_chunk = jnp.arange(S, dtype=jnp.int32) // CHUNK
    scale = DSA_HEAD_DIM ** -0.5
    gather_rows = jax.vmap(lambda table, idx: table[idx])

    def one_block(args):
        q_blk, qi_blk, w_blk, q0 = args
        q_chunk = (q0 + jnp.arange(Q_BLOCK, dtype=jnp.int32)) // CHUNK
        allowed = key_chunk[None, :] <= q_chunk[:, None]
        dots = jnp.einsum('bqhd,bsd->bqhs', qi_blk, k_idx).astype(jnp.float32) * IDX_DIM ** -0.5
        w = w_blk.astype(jnp.float32) * IDX_HEADS ** -0.5
        index_score = jnp.einsum('bqh,bqhs->bqs', w, jax.nn.relu(dots))
        index_score = jnp.where(allowed[None], index_score, NEG_INF)
        _, sel = lax.top_k(index_score, top_k)
        valid = (sel // CHUNK) <= q_chunk[None, :, None]
        k_sel = gather_rows(k, sel)
        v_sel = gather_rows(v, sel)
        qg = q_blk.reshape(B, Q_BLOCK, DSA_KV_HEADS, DSA_GROUP, DSA_HEAD_DIM)
        s = jnp.einsum('bqgnd,bqkgd->bqgnk', qg, k_sel).astype(jnp.float32) * scale
        s = jnp.where(valid[:, :, None, None, :], s, NEG_INF)
        p = jax.nn.softmax(s, axis=-1).astype(v.dtype)
        o = jnp.einsum('bqgnk,bqkgd->bqgnd', p, v_sel)
        return o.reshape(B, Q_BLOCK, DSA_HEADS * DSA_HEAD_DIM)

    out = lax.map(one_block, (to_blocks(q), to_blocks(q_idx), to_blocks(w_idx), starts))
    return from_blocks(out)

def peer_ffn(h, w_q, sub_keys, u_emb, v_emb):
    B, S, D = h.shape
    n_blocks = (B * S) // PEER_TOKEN_BLOCK
    half = PEER_KEY_DIM // 2

    def one_block(xb):
        q = jnp.einsum('td,dhk->thk', xb, w_q).reshape(PEER_TOKEN_BLOCK, PEER_HEADS, 2, half)
        s = jnp.einsum('thpc,hpnc->thpn', q, sub_keys).astype(jnp.float32)
        s1, i1 = lax.top_k(s[:, :, 0], PEER_TOPK)
        s2, i2 = lax.top_k(s[:, :, 1], PEER_TOPK)
        cand_s = (s1[..., :, None] + s2[..., None, :]).reshape(PEER_TOKEN_BLOCK, PEER_HEADS, -1)
        cand_i = (i1[..., :, None] * PEER_N_KEYS + i2[..., None, :]).reshape(PEER_TOKEN_BLOCK, PEER_HEADS, -1)
        top_s, pos = lax.top_k(cand_s, PEER_TOPK)
        expert = jnp.take_along_axis(cand_i, pos, axis=-1)
        g = jax.nn.softmax(top_s, axis=-1)
        u = u_emb[expert]
        a = jax.nn.gelu(jnp.einsum('thkd,td->thk', u, xb).astype(jnp.float32), approximate=False)
        coef = (g * a).astype(xb.dtype)
        return jnp.einsum('thk,thkd->td', coef, v_emb[expert])

    out = lax.map(one_block, h.reshape(n_blocks, PEER_TOKEN_BLOCK, D))
    return out.reshape(B, S, D)

def first_inputs(seed: int = 0) -> dict:
    key = jax.random.key(seed)
    ks = jax.random.split(key, 20)
    f32 = jnp.float32
    L = DEPTH

    def nrm(k, shape, fan_in):
        return jax.random.normal(k, shape, f32) * (fan_in ** -0.5)

    def gain(k, shape):
        return 1.0 + 0.01 * jax.random.normal(k, shape, f32)

    x = jax.random.normal(ks[0], (BATCH, SEQ, D_MODEL), f32)
    start = jax.random.randint(ks[1], (BATCH, 1), 0, 64, dtype=jnp.int32) * CHUNK
    positions = start + jnp.arange(SEQ, dtype=jnp.int32)[None, :]
    return {
        'x': x,
        'positions': positions,
        'norm_mix_g': gain(ks[2], (L, D_MODEL)),
        'w_in': nrm(ks[3], (L, D_MODEL, IN_WIDTH), D_MODEL),
        'mla_q_norm_g': gain(ks[4], (L, MLA_Q_RANK)),
        'mla_kv_norm_g': gain(ks[5], (L, MLA_KV_RANK)),
        'mla_w_uq': nrm(ks[6], (L, MLA_Q_RANK, MLA_HEADS, MLA_NOPE + MLA_ROPE), MLA_Q_RANK),
        'mla_w_uk': nrm(ks[7], (L, MLA_KV_RANK, MLA_HEADS, MLA_NOPE), MLA_KV_RANK),
        'mla_w_uv': nrm(ks[8], (L, MLA_KV_RANK, MLA_HEADS, MLA_V), MLA_KV_RANK),
        'w_branch_a': nrm(ks[9], (L, MLA_HEADS * MLA_V, D_MODEL), MLA_HEADS * MLA_V),
        'w_branch_b': nrm(ks[10], (L, DSA_HEADS * DSA_HEAD_DIM, D_MODEL), DSA_HEADS * DSA_HEAD_DIM),
        'w_out': nrm(ks[11], (L, D_MODEL, D_MODEL), D_MODEL),
        'norm_ffn_g': gain(ks[12], (L, D_MODEL)),
        'peer_w_q': nrm(ks[13], (L, D_MODEL, PEER_HEADS, PEER_KEY_DIM), D_MODEL),
        'peer_sub_keys': nrm(ks[14], (L, PEER_HEADS, 2, PEER_N_KEYS, PEER_KEY_DIM // 2), PEER_KEY_DIM // 2),
        'peer_u': nrm(ks[15], (L, PEER_N_EXPERTS, D_MODEL), D_MODEL),
        'peer_v': nrm(ks[16], (L, PEER_N_EXPERTS, D_MODEL), PEER_HEADS),
        'norm_final_g': gain(ks[17], (D_MODEL,)),
    }

def first_block(x, positions, norm_mix_g, w_in, mla_q_norm_g, mla_kv_norm_g, mla_w_uq, mla_w_uk,
              mla_w_uv, w_branch_a, w_branch_b, w_out, norm_ffn_g, peer_w_q, peer_sub_keys,
              peer_u, peer_v, norm_final_g):
    B, S, _ = x.shape
    splits = [int(c) for c in np.cumsum(IN_SIZES)[:-1]]
    for l in range(DEPTH):
        h = rmsnorm(x, norm_mix_g[l])
        proj = jnp.einsum('bsd,de->bse', h, w_in[l])
        c_q, c_kv, k_rope, dq, dk, dv, iq, ik, iw, gates = jnp.split(proj, splits, axis=-1)
        o_a = mla_branch(c_q, c_kv, k_rope, positions, mla_q_norm_g[l], mla_kv_norm_g[l],
                         mla_w_uq[l], mla_w_uk[l], mla_w_uv[l])
        o_b = dsa_branch(dq, dk, dv, iq, ik, iw, positions)
        gate = jax.nn.sigmoid(gates.astype(jnp.float32)).astype(x.dtype).reshape(B, S, N_BRANCHES, D_MODEL)
        merged = gate[:, :, 0, :] * (o_a @ w_branch_a[l]) + gate[:, :, 1, :] * (o_b @ w_branch_b[l])
        x = x + merged @ w_out[l]
        x = x + peer_ffn(rmsnorm(x, norm_ffn_g[l]), peer_w_q[l], peer_sub_keys[l], peer_u[l], peer_v[l])
    return rmsnorm(x, norm_final_g)


D_MIX = D_MODEL
MLSTM_WIDTH = D_MIX // 2
MLSTM_HEADS = 4
MLSTM_HEAD_DIM = MLSTM_WIDTH // MLSTM_HEADS
MLSTM_CHUNK = 128
CONV_WIDTH = 4
S5_WIDTH = D_MIX - MLSTM_WIDTH
S5_GROUP = 16
S5_GROUPS = S5_WIDTH // S5_GROUP
S5_STATE = 64
S5_DT_MIN = 1e-3
S5_DT_MAX = 1e-1
PEER_NKEYS = 128
PEER_EXPERTS = PEER_NKEYS * PEER_NKEYS
PEER_QDIM = 256
PEER_BLOCK = 128
RMS_EPS = 1e-6
N_IN = 4 * MLSTM_WIDTH + 2 * MLSTM_HEADS + S5_WIDTH


def rmsnorm_2(x, g):
    xf = x.astype(jnp.float32)
    y = xf * lax.rsqrt(jnp.mean(xf * xf, axis=-1, keepdims=True) + RMS_EPS)
    return (y * g.astype(jnp.float32)).astype(x.dtype)

def causal_dwconv(x, w):
    K, C = w.shape
    return lax.conv_general_dilated(
        x, w[:, None, :].astype(x.dtype), window_strides=(1,), padding=((K - 1, 0),),
        dimension_numbers=('NWC', 'WIO', 'NWC'), feature_group_count=C)

def mlstm_chunkwise(q, k, v, li, lf):
    B, H, S, Dh = q.shape
    L = MLSTM_CHUNK
    NC = S // L
    q = q.reshape(B, H, NC, L, Dh) * (Dh ** -0.5)
    k = k.reshape(B, H, NC, L, Dh)
    v = v.reshape(B, H, NC, L, Dh)
    li = li.reshape(B, H, NC, L)
    lf = lf.reshape(B, H, NC, L)
    a = jnp.cumsum(lf, axis=-1)
    A = a[..., -1]
    g = A[..., None] - a + li
    m_loc = jnp.max(g, axis=-1)
    w = jnp.exp(g - m_loc[..., None])
    dC = jnp.einsum('bhcl,bhcld,bhcle->bhcde', w, k, v)
    dn = jnp.einsum('bhcl,bhcld->bhcd', w, k)

    def step(carry, inp):
        C, n, m = carry
        dC_c, dn_c, m_c, A_c = inp
        m_new = jnp.maximum(A_c + m, m_c)
        s_old = jnp.exp(A_c + m - m_new)
        s_new = jnp.exp(m_c - m_new)
        C_new = s_old[..., None, None] * C + s_new[..., None, None] * dC_c
        n_new = s_old[..., None] * n + s_new[..., None] * dn_c
        return (C_new, n_new, m_new), (C, n, m)

    init = (jnp.zeros((B, H, Dh, Dh), jnp.float32), jnp.zeros((B, H, Dh), jnp.float32),
            jnp.zeros((B, H), jnp.float32))
    xs = (jnp.moveaxis(dC, 2, 0), jnp.moveaxis(dn, 2, 0), jnp.moveaxis(m_loc, 2, 0), jnp.moveaxis(A, 2, 0))
    _, (C0, n0, m0) = lax.scan(step, init, xs)
    C0 = jnp.moveaxis(C0, 0, 2)
    n0 = jnp.moveaxis(n0, 0, 2)
    m0 = jnp.moveaxis(m0, 0, 2)

    Dmat = a[..., :, None] - a[..., None, :] + li[..., None, :]
    causal = jnp.tril(jnp.ones((L, L), dtype=bool))
    Dmat = jnp.where(causal, Dmat, -jnp.inf)
    m_inter = a + m0[..., None]
    m_t = jnp.maximum(m_inter, jnp.max(Dmat, axis=-1))
    Wm = jnp.exp(Dmat - m_t[..., None])
    s_inter = jnp.exp(m_inter - m_t)
    qk = jnp.einsum('bhcjd,bhcsd->bhcjs', q, k) * Wm
    num = jnp.einsum('bhcjs,bhcse->bhcje', qk, v) + s_inter[..., None] * jnp.einsum('bhcjd,bhcde->bhcje', q, C0)
    den = jnp.sum(qk, axis=-1) + s_inter * jnp.einsum('bhcjd,bhcd->bhcj', q, n0)
    h = num / jnp.maximum(jnp.abs(den), jnp.exp(-m_t))[..., None]
    return h.reshape(B, H, S, Dh)

def s5_groups(u, lam_re, lam_im, log_dt, b_re, b_im, c_re, c_im, d, glu_w):
    S = u.shape[1]
    f32 = jnp.float32
    lam_re = lam_re.astype(f32); lam_im = lam_im.astype(f32)
    dt = jnp.exp(log_dt.astype(f32))[:, None]
    mag = jnp.exp(lam_re * dt)
    ar = mag * jnp.cos(lam_im * dt)
    ai = mag * jnp.sin(lam_im * dt)
    den = lam_re * lam_re + lam_im * lam_im
    fr = ((ar - 1.0) * lam_re + ai * lam_im) / den
    fi = (ai * lam_re - (ar - 1.0) * lam_im) / den
    b_re = b_re.astype(f32); b_im = b_im.astype(f32)
    bbr = fr[..., None] * b_re - fi[..., None] * b_im
    bbi = fr[..., None] * b_im + fi[..., None] * b_re
    xr = jnp.einsum('bsgh,gph->bsgp', u, bbr)
    xi = jnp.einsum('bsgh,gph->bsgp', u, bbi)
    G, P = ar.shape
    a_r = jnp.broadcast_to(ar[None, None], (1, S, G, P))
    a_i = jnp.broadcast_to(ai[None, None], (1, S, G, P))

    def combine(e1, e2):
        a1r, a1i, b1r, b1i = e1
        a2r, a2i, b2r, b2i = e2
        return (a1r * a2r - a1i * a2i, a1r * a2i + a1i * a2r,
                a2r * b1r - a2i * b1i + b2r, a2r * b1i + a2i * b1r + b2i)

    _, _, sr, si = lax.associative_scan(combine, (a_r, a_i, xr, xi), axis=1)
    y = (jnp.einsum('bsgp,ghp->bsgh', sr, c_re.astype(f32))
         - jnp.einsum('bsgp,ghp->bsgh', si, c_im.astype(f32))
         + d.astype(f32) * u)
    ab = jnp.einsum('bsgh,ghk->bsgk', jax.nn.gelu(y, approximate=False), glu_w.astype(f32))
    return ab[..., :S5_GROUP] * jax.nn.sigmoid(ab[..., S5_GROUP:])

def peer(x, wq, subkeys, u_tab, v_tab):
    B, S, D = x.shape
    f32 = jnp.float32
    half = PEER_QDIM // 2
    q = (x @ wq).astype(f32).reshape(B, S, PEER_HEADS, 2, half)
    s = jnp.einsum('bshpd,pkd->bshpk', q, subkeys.astype(f32))
    s1, i1 = lax.top_k(s[..., 0, :], PEER_TOPK)
    s2, i2 = lax.top_k(s[..., 1, :], PEER_TOPK)
    cand_s = (s1[..., :, None] + s2[..., None, :]).reshape(B, S, PEER_HEADS, PEER_TOPK * PEER_TOPK)
    cand_i = (i1[..., :, None] * PEER_NKEYS + i2[..., None, :]).reshape(B, S, PEER_HEADS, PEER_TOPK * PEER_TOPK)
    top_s, pos = lax.top_k(cand_s, PEER_TOPK)
    idx = jnp.take_along_axis(cand_i, pos, axis=-1)
    gate = jax.nn.softmax(top_s, axis=-1)
    T = B * S
    HK = PEER_HEADS * PEER_TOPK
    xb = x.reshape(T // PEER_BLOCK, PEER_BLOCK, D)
    ib = idx.reshape(T // PEER_BLOCK, PEER_BLOCK, HK)
    gb = gate.reshape(T // PEER_BLOCK, PEER_BLOCK, HK)

    def block(args):
        xt, it, gt = args
        ue = jnp.take(u_tab, it, axis=0)
        ve = jnp.take(v_tab, it, axis=0)
        act = jax.nn.gelu(jnp.einsum('td,ted->te', xt, ue).astype(f32), approximate=False)
        return jnp.einsum('te,ted->td', (gt * act).astype(ve.dtype), ve)

    out = lax.map(block, (xb, ib, gb))
    return out.reshape(B, S, D)

def second_inputs(seed: int = 0) -> dict:
    key = jax.random.key(seed)
    ks = jax.random.split(key, 24)
    f32 = jnp.float32
    nrm = lambda k, shape, s: jax.random.normal(k, shape, f32) * s
    L = DEPTH
    G, P, Hg = S5_GROUPS, S5_STATE, S5_GROUP
    f_bias = jnp.broadcast_to(jnp.linspace(3.0, 6.0, MLSTM_HEADS, dtype=f32), (L, MLSTM_HEADS))
    b_gates = jnp.concatenate([nrm(ks[3], (L, MLSTM_HEADS), 0.1),
                               f_bias + nrm(ks[4], (L, MLSTM_HEADS), 0.1)], axis=-1)
    lam_im0 = jnp.pi * jnp.arange(P, dtype=f32)
    log_dt = jax.random.uniform(ks[8], (L, G), f32, math.log(S5_DT_MIN), math.log(S5_DT_MAX))
    return dict(
        x=nrm(ks[0], (BATCH, SEQ, D_MODEL), 1.0),
        norm1_g=1.0 + nrm(ks[1], (L, D_MODEL), 0.1),
        w_in=nrm(ks[2], (L, D_MODEL, N_IN), D_MODEL ** -0.5),
        b_gates=b_gates,
        conv_qk_w=nrm(ks[5], (L, CONV_WIDTH, 2 * MLSTM_WIDTH), CONV_WIDTH ** -0.5),
        mlstm_norm_g=1.0 + nrm(ks[6], (L, MLSTM_WIDTH), 0.1),
        s5_lambda_re=-0.5 + nrm(ks[7], (L, G, P), 0.01),
        s5_lambda_im=lam_im0 + nrm(ks[9], (L, G, P), 0.01),
        s5_log_dt=log_dt,
        s5_b_re=nrm(ks[10], (L, G, P, Hg), (2 * Hg) ** -0.5),
        s5_b_im=nrm(ks[11], (L, G, P, Hg), (2 * Hg) ** -0.5),
        s5_c_re=nrm(ks[12], (L, G, Hg, P), P ** -0.5),
        s5_c_im=nrm(ks[13], (L, G, Hg, P), P ** -0.5),
        s5_d=nrm(ks[14], (L, G, Hg), 0.5),
        s5_glu_w=nrm(ks[15], (L, G, Hg, 2 * Hg), Hg ** -0.5),
        w_out=nrm(ks[16], (L, D_MIX, D_MODEL), D_MIX ** -0.5),
        norm2_g=1.0 + nrm(ks[17], (L, D_MODEL), 0.1),
        peer_wq=nrm(ks[18], (L, D_MODEL, PEER_HEADS * PEER_QDIM), D_MODEL ** -0.5),
        peer_subkeys=nrm(ks[19], (L, 2, PEER_NKEYS, PEER_QDIM // 2), (PEER_QDIM // 2) ** -0.5),
        peer_u=nrm(ks[20], (L, PEER_EXPERTS, D_MODEL), D_MODEL ** -0.5),
        peer_v=nrm(ks[21], (L, PEER_EXPERTS, D_MODEL), PEER_HEADS ** -0.5),
        final_g=1.0 + nrm(ks[22], (D_MODEL,), 0.1),
    )

def second_block(x, norm1_g, w_in, b_gates, conv_qk_w, mlstm_norm_g, s5_lambda_re, s5_lambda_im,
              s5_log_dt, s5_b_re, s5_b_im, s5_c_re, s5_c_im, s5_d, s5_glu_w, w_out, norm2_g,
              peer_wq, peer_subkeys, peer_u, peer_v, final_g):
    B, S, _ = x.shape
    f32 = jnp.float32
    W, H, Dh = MLSTM_WIDTH, MLSTM_HEADS, MLSTM_HEAD_DIM
    h = x
    for l in range(DEPTH):
        xn = rmsnorm_2(h, norm1_g[l])
        z = xn @ w_in[l]
        q, k, v, o, gates, u = jnp.split(z, [W, 2 * W, 3 * W, 4 * W, 4 * W + 2 * H], axis=-1)
        qk = jax.nn.silu(causal_dwconv(jnp.concatenate([q, k], axis=-1), conv_qk_w[l]))
        q, k = qk[..., :W], qk[..., W:]
        to_heads = lambda t: t.astype(f32).reshape(B, S, H, Dh).transpose(0, 2, 1, 3)
        gates = gates.astype(f32) + b_gates[l].astype(f32)
        li = gates[..., :H].transpose(0, 2, 1)
        lf = jax.nn.log_sigmoid(gates[..., H:]).transpose(0, 2, 1)
        hm = mlstm_chunkwise(to_heads(q), to_heads(k), to_heads(v), li, lf)
        hm = hm.transpose(0, 2, 1, 3)
        hm = hm * lax.rsqrt(jnp.mean(hm * hm, axis=-1, keepdims=True) + RMS_EPS)
        hm = hm.reshape(B, S, W) * mlstm_norm_g[l].astype(f32) * jax.nn.sigmoid(o.astype(f32))
        ys = s5_groups(u.astype(f32).reshape(B, S, S5_GROUPS, S5_GROUP),
                       s5_lambda_re[l], s5_lambda_im[l], s5_log_dt[l], s5_b_re[l], s5_b_im[l],
                       s5_c_re[l], s5_c_im[l], s5_d[l], s5_glu_w[l]).reshape(B, S, S5_WIDTH)
        mix = jnp.concatenate([hm, ys], axis=-1).astype(h.dtype) @ w_out[l]
        h = h + mix.astype(h.dtype)
        h = h + peer(rmsnorm_2(h, norm2_g[l]), peer_wq[l], peer_subkeys[l], peer_u[l], peer_v[l]).astype(h.dtype)
    return rmsnorm_2(h, final_g)


def setup_inputs(seed=0):
    out = dict(first_inputs(seed))
    for name, value in second_inputs(seed + 1).items():
        if name != "x":
            out[name + "_2"] = value
    return out


def reference(
    x, positions, norm_mix_g, w_in, mla_q_norm_g, mla_kv_norm_g, mla_w_uq, mla_w_uk, mla_w_uv,
    w_branch_a, w_branch_b, w_out, norm_ffn_g, peer_w_q, peer_sub_keys, peer_u, peer_v,
    norm_final_g, norm1_g_2, w_in_2, b_gates_2, conv_qk_w_2, mlstm_norm_g_2, s5_lambda_re_2,
    s5_lambda_im_2, s5_log_dt_2, s5_b_re_2, s5_b_im_2, s5_c_re_2, s5_c_im_2, s5_d_2, s5_glu_w_2,
    w_out_2, norm2_g_2, peer_wq_2, peer_subkeys_2, peer_u_2, peer_v_2, final_g_2,
):
    x = first_block(
        x, positions, norm_mix_g, w_in, mla_q_norm_g, mla_kv_norm_g, mla_w_uq, mla_w_uk,
        mla_w_uv, w_branch_a, w_branch_b, w_out, norm_ffn_g, peer_w_q, peer_sub_keys, peer_u,
        peer_v, norm_final_g,
    )
    return second_block(
        x, norm1_g_2, w_in_2, b_gates_2, conv_qk_w_2, mlstm_norm_g_2, s5_lambda_re_2,
        s5_lambda_im_2, s5_log_dt_2, s5_b_re_2, s5_b_im_2, s5_c_re_2, s5_c_im_2, s5_d_2,
        s5_glu_w_2, w_out_2, norm2_g_2, peer_wq_2, peer_subkeys_2, peer_u_2, peer_v_2,
        final_g_2,
    )


_drawn_inputs = setup_inputs


def setup_inputs(seed=0):
    import zlib

    import numpy as np

    out = dict(_drawn_inputs(seed))
    spreads = {}
    factors = {}
    for name, (base, spread) in spreads.items():
        noise = np.random.default_rng([zlib.crc32(name.encode()), seed]).standard_normal(out[name].shape)
        drawn = base * np.exp(spread * noise) if base else spread * noise
        out[name] = __import__('jax').numpy.asarray(drawn.astype(out[name].dtype))
    for name, factor in factors.items():
        out[name] = (out[name] * factor).astype(out[name].dtype)
    return out
```

```python
import math
from contextlib import ExitStack

import numpy as np

import concourse.bass as bass
from concourse import mybir

F32 = mybir.dt.float32
F32R = mybir.dt.float32r
I32 = mybir.dt.int32
U32 = mybir.dt.uint32
ALU = mybir.AluOpType
ACT = mybir.ActivationFunctionType
AX = mybir.AxisListType

P = 128
T = 256
QT = T // P
D = 2048
KT = D // P
CHUNK = 64
EPS = 1e-6
NEG = -1e30
EXP_TILE, SLOTS_TILE = 52, 56
REPLACED = -3e38
ROPE_THETA = 500000.0

MLA_HEADS, MLA_NOPE, MLA_ROPE, MLA_V, Q_RANK, KV_RANK = 8, 128, 64, 128, 512, 256
DSA_HEADS, DSA_KV, HEAD = 8, 2, 128
IDX_HEADS, IDX_DIM = 16, 64
TOPK = T // 4
PEER_HEADS, PEER_K, NKEYS = 8, 16, 128

SQ_BASE = [0, 4, 5, 6, 10, 14, 18, 22]

MLSTM_HEADS, MLSTM_DIM, S5_GROUP, S5_STATE = 4, 256, 16, 64
S5_TILES = 32

CQ, CKV, KI, DQ, DK, DV, IQ, IW, N_PROJ1 = 0, 4, 6, 7, 15, 17, 19, 27, 28
STAGES = [("proj1", 28), ("gates1", 32), ("branch1", 16), ("out1", 16), ("wq1", 8), ("u1", 128), ("v1", 128),
          ("z2", 41), ("out2", 16), ("wq2", 16), ("u2", 128), ("v2", 128)]


def tile_bases():
    base, evac, b, e = {}, {}, 0, 0
    for name, n in STAGES:
        base[name], evac[name] = b, e
        b += n
        e += 0 if name[0] == "v" else n
    return base, evac


def rope_and_masks():
    def rot(block, half):
        m = np.zeros((P, P), np.float32)
        for b in range(0, P, block):
            for i in range(half):
                m[b + half + i, b + i] = -1.0
                m[b + i, b + half + i] = 1.0
        return m

    def place(src, dst):
        m = np.zeros((P, P), np.float32)
        for i in range(64):
            m[src + i, dst + i] = 1.0
        return m

    mla, dsa, idx = rot(64, 32), rot(128, 16), rot(64, 8)
    ka, kb, ia, ib = place(0, 0), place(0, 64), place(64, 0), place(64, 64)
    mats = [mla, dsa, idx, ka, ka @ mla, kb, kb @ mla, ia, ia @ idx, ib, ib @ idx]
    freq = np.zeros((P, 3), np.float32)
    for kind, (block, rotated) in enumerate([(64, 64), (128, 32), (64, 16)]):
        half = rotated // 2
        inv = (np.float32(ROPE_THETA) ** (-(np.arange(half, dtype=np.float32) * 2.0) / np.float32(rotated))).astype(np.float32)
        for p in range(P):
            if p % block < rotated:
                freq[p, kind] = inv[(p % block) % half]
    q = np.arange(T)[:, None] // CHUNK
    k = np.arange(T)[None, :] // CHUNK
    mask = np.where(k <= q, 0.0, NEG).astype(np.float32).reshape(QT, P, T)
    return (np.ascontiguousarray(np.stack(mats).transpose(1, 0, 2)), freq,
            np.ascontiguousarray(mask.transpose(1, 0, 2)))


def build_two_blocks(nc, a):
    base, evac = tile_bases()
    nstage = dict(STAGES)

    with ExitStack() as ctx:
        def sb(name, shape, dt=F32):
            return ctx.enter_context(nc.sbuf_tensor("sb_" + name, shape, dt))

        def sem(name):
            return ctx.enter_context(nc.semaphore(name))

        act_hl = sb("act_hl", [P, KT, 2 * T], F32R)
        w_hi = sb("w_hi", [P, 4, 512], F32R)
        w_lo = sb("w_lo", [P, 4, 512], F32R)
        raw = sb("raw", [P, 4, 1024])
        work = sb("work", [P, 128, T])
        consts = sb("consts", [P, 3, P])
        cols = sb("cols", [P, a["cols"].shape[1]])
        slots = sb("slots", [P, 3, T])
        scratch = sb("scratch", [P, 8, T])
        psum = ctx.enter_context(nc.psum_tensor("psum", [P, 8, 512], F32))
        ident, iota, ones = consts[:, 0, :], consts[:, 1, :], consts[:, 2, :]
        x_mid = nc.dram_tensor("x_mid", [P, KT, T], F32, kind="Internal").ap()

        def rows(lo, hi):
            return work[:, lo:hi, :]

        def flat(lo, hi):
            return work[:, lo:hi, :].rearrange("p r c -> p (r c)")

        c_mix, c_qn, c_kvn, c_ffn, c_fin, c_freq = (
            cols[:, lo:hi] for lo, hi in ((0, 16), (16, 20), (20, 22), (22, 38), (38, 54), (54, 57)))
        (c_n1, c_mlstm, c_n2, c_fin2, c_bias, c_half_pi, c_pair, c_eight, c_d) = (
            cols[:, lo:hi] for lo, hi in ((57, 73), (73, 81), (81, 97), (97, 113), (113, 114), (114, 115), (115, 117), (117, 125), (125, 133)))
        c_conv = cols[:, 133:197].rearrange("p (k j) -> p k j", j=4)

        stat = scratch[:, 0:3, :]
        gate_tmp = sb("gate_tmp", [P, 2, P, 2])
        onehot = scratch.rearrange("p (s h) (b n) -> p s (h b) n", s=2, n=P)

        x_t, tmp = rows(0, 16), rows(16, 32)
        proj = rows(32, 60)
        w_uq = flat(60, 84).rearrange("p (k n) -> p k n", k=4)
        w_uk = flat(84, 92).rearrange("p (k n) -> p k n", k=2)
        w_uv = flat(92, 100).rearrange("p (k n) -> p k n", k=2)
        q_nope, q_rope, k_nope = rows(100, 108), rows(108, 112), rows(112, 120)
        v_row = flat(120, 128).rearrange("p (t n) -> p t n", t=QT)
        low_sq = rows(100, 106)
        pos_i, pos_f, turns = rows(100, 101), rows(101, 102), rows(102, 105)
        rope_s, rope_c = slots[:, :, :], scratch[:, 3:6, :]
        mats = flat(9, 15)[:, 0:11 * P].rearrange("p (m c) -> p m c", c=P)
        k_pe, ik = rows(25, 27), rows(17, 19)
        mask = rows(19, 21)
        dv_row = rows(21, 23)
        select = rows(23, 25)
        rot_tmp = rows(15, 17)
        s_sb = flat(95, 100)[:, 0:9 * P].rearrange("p (b n) -> p b n", b=3)
        p_t = flat(92, 95).rearrange("p (b n) -> p b n", b=2)
        iw_row = flat(31, 32)[:, 0:32].rearrange("p (t h) -> p t h", t=QT)
        small, soft_c = flat(31, 32)[:, 64:80], flat(31, 32)[:, 80:96].rearrange("p (b n t) -> p b n t", b=2, t=QT)
        relu = flat(92, 100)
        o_heads = rows(60, 76)
        gates, merged, x1 = [rows(76, 92), rows(0, 16)], rows(0, 16), rows(32, 48)

        h_ffn = rows(48, 64)
        peer_keys1 = rows(16, 24)
        peer_q = rows(64, 80)
        route_out = flat(80, 83).rearrange("p (t j s) -> p t j s", t=QT, j=3)
        ch_i = flat(83, 84)[:, 0:128].bitcast(U32).rearrange("p (h k) -> p h k", k=PEER_K)
        ch_b = flat(83, 84)[:, 128:256].bitcast(U32).rearrange("p (h k) -> p h k", k=PEER_K)
        key_scores = [flat(lo, lo + 8).rearrange("p (g n) -> p g n", n=NKEYS) for lo in (84, 116)]
        key_work = flat(92, 100).rearrange("p (g n) -> p g n", n=NKEYS)
        cand, cand_work = rows(100, 108), rows(108, 116)
        eq = flat(64, 72).rearrange("p (h k a) -> p h k a", h=PEER_HEADS, k=PEER_K)
        rs = flat(124, 128)
        top_v = rs[:, 0:256].rearrange("p (g k) -> p g k", k=PEER_K)
        top_i = rs[:, 256:512].bitcast(U32).rearrange("p (g k) -> p g k", k=PEER_K)
        top_f = rs[:, 512:768].rearrange("p (g k) -> p g k", k=PEER_K)
        ch_v = rs[:, 768:896].rearrange("p (h k) -> p h k", k=PEER_K)
        ch_f = rs[:, 896:1024].rearrange("p (h k) -> p h k", k=PEER_K)
        ch_e = flat(72, 73).rearrange("p (t h k) -> p t h k", t=QT, k=PEER_K)
        ch_s = flat(73, 74).rearrange("p (t n) -> p t n", t=QT)
        gate_e = work[:, :, :]

        xb, qk = rows(0, 16), rows(0, 16)
        xn = rows(32, 48)
        z = rows(32, 73)
        z_u, z_g, z_qk, z_v, z_o = rows(32, 40), rows(40, 41), rows(41, 57), rows(57, 65), rows(65, 73)
        mix = rows(16, 32)
        v_one = flat(73, 82)[:, 0:QT * 4 * 257].rearrange("p (c h n) -> p c h n", c=QT, h=4)
        state = flat(82, 91)[:, 0:8 * 257].rearrange("p (g n) -> p g n", g=8)
        nums = flat(91, 100)[:, 0:8 * 257].rearrange("p (u n) -> p u n", u=8)
        k_w = flat(100, 104)
        diag = flat(104, 108).rearrange("p (u n) -> p u n", n=P)
        decay = flat(108, 112).rearrange("p (u n) -> p u n", n=P)
        p_m, pt_m = flat(112, 113).rearrange("p (b n) -> p b n", n=P), flat(113, 114).rearrange("p (b n) -> p b n", n=P)
        tiny = flat(114, 116)
        tri, causal = flat(127, 128)[:, 0:P], flat(127, 128)[:, P:2 * P]
        nums_sq = flat(100, 108)
        s5v = flat(96, 98).rearrange("p (n g) -> p n g", g=S5_TILES)
        b_raw = [flat(lo, lo + 2).rearrange("p (g h) -> p g h", h=16) for lo in (32, 34)]
        c_raw = [flat(lo, lo + 2).rearrange("p (g h) -> p g h", h=16) for lo in (36, 38)]
        b_bar = [flat(lo, lo + 2).rearrange("p (g h) -> p g h", h=16) for lo in (40, 42)]
        b_tmp = flat(44, 46).rearrange("p (g h) -> p g h", h=16)
        b_blk = [flat(48, 52), flat(52, 56)]
        b_in = [flat(74, 78).rearrange("p (j s) -> p j s", s=P), flat(78, 82).rearrange("p (j s) -> p j s", s=P)]
        c_blk = [flat(82, 86), flat(86, 90), flat(90, 94)]
        cos_t = [rows(98, 102), rows(102, 106)]
        sin_t = [rows(106, 110), rows(110, 114)]
        turn_t, near_t = rows(114, 118), rows(118, 122)
        x_cos, x_sin = rows(122, 124), rows(124, 126)
        x_rot, s_rot = rows(16, 18), rows(28, 32)
        y_cos, y_sin = rows(20, 24), rows(24, 28)
        glu_raw = flat(94, 95).rearrange("p (j n) -> p j n", n=32)
        glu_w = [flat(82, 86).rearrange("p (j n) -> p j n", n=P), flat(86, 90).rearrange("p (j n) -> p j n", n=P)]
        y_g = z_u
        peer_keys2 = flat(16, 17).rearrange("p (q n) -> p q n", q=2)

        x_loaded = [sem(f"x_loaded{c}") for c in range(4)]
        consts_loaded, small_loaded = sem("consts_loaded"), sem("small_loaded")
        keys_clear, keys_loaded = sem("keys_clear"), sem("keys_loaded")
        gates_ready, gated, merged_ready = sem("gates_ready"), sem("gated"), sem("merged_ready")
        pos_loaded = sem("pos_loaded")
        raw_loaded = [sem(f"raw_loaded{j}") for j in range(4)]
        hi_ready, lo_ready = sem("hi_ready"), sem("lo_ready")
        quarter_used = sem("quarter_used")
        tile_out = sem("tile_out")
        sq_ready, sum_ready, mean_ready, root_ready = sem("sq_ready"), sem("sum_ready"), sem("mean_ready"), sem("root_ready")
        act_ready = sem("act_ready")
        dve_step = sem("dve_step")
        norm_ready = sem("norm_ready")
        up_done, up_out = sem("up_done"), sem("up_out")
        angle_ready, sin_ready = sem("angle_ready"), sem("sin_ready")
        rot_done, rot_used = sem("rot_done"), sem("rot_used")
        turn_done, turn_out = sem("turn_done"), sem("turn_out")
        dots_done, relu_done, dots_used = sem("dots_done"), sem("relu_done"), sem("dots_used")
        s_done, s_shifted, p_exp, p_ready = sem("s_done"), sem("s_shifted"), sem("p_exp"), sem("p_ready")
        pt_done, pt_ready, o_done, o_ready = sem("pt_done"), sem("pt_ready"), sem("o_done"), sem("o_ready")
        x_again = sem("x_again")
        x_kept = sem("x_kept")
        out_stored = sem("out_stored")
        scores_done, scores_out, route_done = sem("scores_done"), sem("scores_out"), sem("route_done")
        gate_exp_in, gate_exp = sem("gate_exp_in"), sem("gate_exp")
        slots_done, slots_ready = sem("slots_done"), sem("slots_ready")
        hot_ready, hot_used, gate_out = sem("hot_ready"), sem("hot_used"), sem("gate_out")
        weighed = sem("weighed")
        c_hi, c_lo = sem("c_hi"), sem("c_lo")
        block_in, conv_done = sem("block_in"), sem("conv_done")
        masks_loaded, s5_loaded, glu_loaded = sem("masks_loaded"), sem("s5_loaded"), sem("glu_loaded")
        qk_ready, o_gate_ready = sem("qk_ready"), sem("o_gate_ready")
        vt_done, vt_out = sem("vt_done"), sem("vt_out")
        gate_bias, gt_done = sem("gate_bias"), sem("gt_done")
        ml_in, ml_out = sem("ml_in"), sem("ml_out")
        lf_ready, cum_done = sem("lf_ready"), sem("cum_done")
        diag_ready, row_done = sem("diag_ready"), sem("row_done")
        decay_in, decay_ready = sem("decay_in"), sem("decay_ready")
        kt_done, kw_ready = sem("kt_done"), sem("kw_ready")
        st_done, st_out = sem("st_done"), sem("st_out")
        qk_done, pm_ready = sem("qk_done"), sem("pm_ready")
        pmt_done, pmt_ready = sem("pmt_done"), sem("pmt_ready")
        num_done, num_out, inter_done, inter_out = sem("num_done"), sem("num_out"), sem("inter_done"), sem("inter_out")
        hm_ready, hmt_done, hmt_out = sem("hm_ready"), sem("hmt_done"), sem("hmt_out")
        s5_in, s5_out = sem("s5_in"), sem("s5_out")
        blk_ready, bt_done, bt_out = sem("blk_ready"), sem("bt_done"), sem("bt_out")
        table_in, table_ready = sem("table_in"), sem("table_ready")
        xs_done, xs_used, s_ready = sem("xs_done"), sem("xs_used"), sem("s_ready")
        ys_in, ys_done, ys_out, y_gelu = sem("ys_in"), sem("ys_done"), sem("ys_out"), sem("y_gelu")
        glu_ready, glu_done, glu_sig, glu_out = sem("glu_ready"), sem("glu_done"), sem("glu_sig"), sem("glu_out")

        rots = [(proj[:, IQ + 2 * j:IQ + 2 * j + 2], 2) for j in range(4)] + [(2, 2), (3, 2)]
        rots += [(q_rope[:, 0:2], 0), (q_rope[:, 2:4], 0), (0, 0), (1, 0)]
        rots += [(proj[:, DQ + 2 * j:DQ + 2 * j + 2], 1) for j in range(4)] + [(proj[:, DK:DK + 2], 1)]
        N_IDX_ROT, N_MLA_ROT, N_ROT = 6, 10, 15
        ATTENTION_STEPS = 31

        def rots_of(step):
            return [2 * step, 2 * step + 1] if step < 3 else [step + 3] if step < 12 else []

        def in_step(step, first, n):
            return [step - first] if 0 <= step - first < n else []

        block = ctx.enter_context(nc.Block())

        def tiles(eng, first, last, body):
            turns = (last - first) // 2
            if turns > 0:
                with eng.Fori(0, turns) as turn:
                    body(turn * 2 + first, 0)
                    body(turn * 2 + (first + 1), 1)
            if (last - first) % 2:
                body(first + 2 * turns, 0)

        def bank_of(b, first, u):
            return (b + first + u) % 2

        def experts(pe, blk, sum_squares, gemm, quarter):
            sum_squares({1: 3, 2: 6}[blk], rows(0, 16), 16)
            gemm(f"wq{blk}", acts={1: 4, 2: 7}[blk])
            pe.wait_ge(tile_out, evac[f"u{blk}"])
            pe.wait_ge(keys_loaded, {1: 32, 2: 48}[blk])
            u = 16 * (blk - 1)
            for t in range(QT):
                for h in range(PEER_HEADS):
                    if u >= 2:
                        pe.wait_ge(scores_out, u - 1)
                    if blk == 1:
                        mm = pe.matmul(psum[:, 2 + u % 2, 0:T], peer_q[:, h, t * P:t * P + P], peer_keys1[:, h, :],
                                       start=True, stop=True)
                    else:
                        for q in range(2):
                            mm = pe.matmul(psum[:, 2 + u % 2, q * P:q * P + P], peer_q[:, 2 * h + q, t * P:t * P + P],
                                           peer_keys2[:, q, :], start=True, stop=True)
                    mm.then_inc(scores_done, 1)
                    u += 1

            def turn_slots():
                pe.wait_ge(route_done, blk)
                for t in range(QT):
                    for j in range(3):
                        mm = pe.transpose(psum[:, 4 + t, j * P:j * P + P], route_out[:, t, j, :], ident)
                    mm.then_inc(slots_done, 1)

            gemm(f"u{blk}", between={SLOTS_TILE: turn_slots})
            pe.wait_ge(slots_ready, 2 * blk)
            h0 = 64 * (blk - 1)

            def hot(g, half, wait):
                pe.wait_ge(hot_ready, g + (h0 + 1))
                if wait:
                    pe.wait_ge(gate_out, g * 2 + (2 * h0 - 2))
                for j in range(4):
                    mm = pe.matmul(psum[:, 6 + half, j * P:j * P + P], onehot[:, 0, 4 * half + j, :], onehot[:, 1, 4 * half + j, :],
                                   start=True, stop=True)
                mm.then_inc(hot_used, 1)

            if blk == 1:
                hot(0, 0, False)
                hot(1, 1, False)
            tiles(pe, 2 if blk == 1 else 0, 64, lambda g, u: hot(g, u, True))
            pe.wait_ge(tile_out, evac[f"u{blk}"] + 128)
            pe.wait_ge(gate_out, 128 * blk)
            b = base[f"v{blk}"]

            def out_tile(i, par, first):
                pe.wait_ge(c_lo, i + (128 * (blk - 1) + 1))
                for c in range(4):
                    pe.wait_ge(lo_ready, (i + b) * 4 + c + 1)
                    for kk in range(4):
                        m = 4 * c + kk
                        ps = psum[:, m // 2, (m % 2) * T:(m % 2) * T + T]
                        w_h, w_l = w_hi[:, c, kk * P:kk * P + P], w_lo[:, c, kk * P:kk * P + P]
                        pe.matmul(ps, w_h, act_hl[:, par, 0:T], start=first and m % 2 == 0, stop=False, skip_group_check=True)
                        pe.matmul(ps, w_h, act_hl[:, par, T:2 * T], start=False, stop=False, skip_group_check=True)
                        mm = pe.matmul(ps, w_l, act_hl[:, par, 0:T], start=False, stop=False, skip_group_check=True)
                    mm.then_inc(quarter_used, 1)

            out_tile(0, 0, True)
            tiles(pe, 1, 128, lambda i, u: out_tile(i, (1 + u) % 2, False))

        def act_experts(act, blk, root, begin, stage, plain, split):
            begin(f"wq{blk}")
            root({1: 3, 2: 6}[blk])
            if blk == 1:
                act.wait_ge(keys_clear, 1)
                act.dma_start(peer_keys1[0:64, :, 0:P], a["keys1"][0:64]).then_inc(keys_loaded, 16)
                act.dma_start(peer_keys1[64:P, :, P:T], a["keys1"][64:P]).then_inc(keys_loaded, 16)
            else:
                act.wait_ge(act_ready, 28)
                act.dma_start(peer_keys2, a["keys2"]).then_inc(keys_loaded, 16)
            stage(f"wq{blk}", plain(f"wq{blk}", peer_q), begun=True)
            u = 16 * (blk - 1)
            for t in range(QT):
                for h in range(PEER_HEADS):
                    act.wait_ge(scores_done, u + 1)
                    act.copy(key_scores[t][:, 2 * h:2 * h + 2, :], psum[:, 2 + u % 2, 0:T].rearrange("p (q n) -> p q n", q=2)).then_inc(scores_out, 1)
                    u += 1
            act.wait_ge(x_kept, {1: 16, 2: 48}[blk])

            def exponentials():
                act.wait_ge(gate_exp_in, QT * blk)
                act.activation(ch_e, ch_e, ACT.Exp).then_inc(gate_exp, 1)

            def keep_slots():
                for t in range(QT):
                    act.wait_ge(slots_done, QT * (blk - 1) + t + 1)
                    act.copy(slots[:, :, t * P:t * P + P], psum[:, 4 + t, 0:3 * P].rearrange("p (j s) -> p j s", j=3)).then_inc(slots_ready, 1)

            def gelu(i, par):
                act.wait_ge(quarter_used, (i + base[f"u{blk}"]) * 4 + 4)
                act.activation(gate_e[:, i, :], psum[:, par, 0:T], ACT.Gelu).then_inc(tile_out, 1)

            stage(f"u{blk}", gelu, between={EXP_TILE: exponentials, SLOTS_TILE: keep_slots})
            h0 = 64 * (blk - 1)

            def gather(g, half, wait):
                act.wait_ge(hot_used, g + (h0 + 1))
                for q in range(2):
                    if wait:
                        act.wait_ge(weighed, g * 2 + (2 * h0 + q - 1))
                    act.copy(gate_tmp[:, q], psum[:, 6 + half, q * T:q * T + T].rearrange("p (t n) -> p n t", t=2)).then_inc(gate_out, 1)

            gather(0, 0, False)
            tiles(act, 1, 64, lambda g, u: gather(g, (1 + u) % 2, True))
            act.wait_ge(weighed, 128 * blk)
            b = base[f"v{blk}"]
            act.wait_ge(quarter_used, 4 * b)
            act.wait_ge(tile_out, evac[f"u{blk}"] + 128)

            def high(i, u):
                par = (b + u) % 2
                act.wait_ge(quarter_used, i * 4 + (4 * b - 4))
                act.copy(act_hl[:, u, 0:T], gate_e[:, i, :]).then_inc(c_hi, 1)
                split(i + b, par, True)

            if blk == 1:
                tiles(act, 0, 100, high)
                act_s5_loads(act)
                tiles(act, 100, 106, high)
                act_s5_decay(act)
                tiles(act, 106, 108, high)
                act_s5_turn(act)
                tiles(act, 108, 128, high)
            else:
                tiles(act, 0, 128, high)

        def dve_experts(dve, blk, link, rms, split_act, low, stage):
            dve.wait_ge(tile_out, evac[f"wq{blk}"])
            rms({1: 3, 2: 6}[blk], x1, 16, D, {1: c_ffn, 2: c_n2}[blk], h_ffn, rows(0, 16), begun=f"wq{blk}")
            split_act(h_ffn, 4 * base[f"wq{blk}"], norm=True)
            stage(f"wq{blk}")

            def top16(v, i, s, w, groups):
                some = PEER_HEADS
                for lo in range(0, groups, some):
                    for g in range(lo, lo + some):
                        ins = dve.max(v[:, g, 0:8], s[:, g, :])
                    link(ins)
                    yield
                for lo in range(0, groups, some):
                    for g in range(lo, lo + some):
                        dve.max_index(i[:, g, 0:8], v[:, g, 0:8], s[:, g, :])
                    yield
                    for g in range(lo, lo + some):
                        ins = dve.match_replace(w[:, g, :], v[:, g, 0:8], s[:, g, :], REPLACED)
                    link(ins)
                    yield
                for lo in range(0, groups, some):
                    for g in range(lo, lo + some):
                        ins = dve.max(v[:, g, 8:16], w[:, g, :])
                    link(ins)
                    yield
                for lo in range(0, groups, some):
                    for g in range(lo, lo + some):
                        ins = dve.max_index(i[:, g, 8:16], v[:, g, 8:16], w[:, g, :])
                    link(ins)
                    yield

            top4 = top_v.rearrange("p (h q) k -> p h q k", q=2)
            topf4 = top_f.rearrange("p (h q) k -> p h q k", q=2)
            cube = [P, PEER_HEADS, PEER_K, PEER_K]

            def choose():
                for t in range(QT):
                    if t == 0:
                        dve.wait_ge(scores_out, 16 * blk)
                    yield from top16(top_v, top_i, key_scores[t], key_work, 16)
                    link(dve.tensor_copy(top_f, top_i))
                    link(dve.tensor_tensor(cand.rearrange("p h (x y) -> p h x y", x=PEER_K), top4[:, :, 0, :].unsqueeze(3).broadcast_to(cube),
                                           top4[:, :, 1, :].unsqueeze(2).broadcast_to(cube), ALU.add))
                    yield
                    yield from top16(ch_v, ch_i, cand, cand_work, PEER_HEADS)
                    dve.tensor_tensor(ch_e[:, t], ch_v, ch_v[:, :, 0:1].broadcast_to([P, PEER_HEADS, PEER_K]), ALU.subtract).then_inc(gate_exp_in, 1)
                    dve.tensor_scalar(ch_b, ch_i, 15, None, ALU.bitwise_and)
                    link(dve.tensor_scalar(ch_i, ch_i, 4, None, ALU.logical_shift_right))
                    for q, place in enumerate((ch_i, ch_b)):
                        link(dve.tensor_copy(ch_f, place))
                        link(dve.tensor_tensor(eq, iota[:, 0:PEER_K].unsqueeze(1).unsqueeze(1).broadcast_to(cube),
                                               ch_f.unsqueeze(3).broadcast_to(cube), ALU.is_equal))
                        yield
                        link(dve.tensor_tensor(eq, eq, topf4[:, :, q, :].unsqueeze(2).broadcast_to(cube), ALU.mult))
                        yield
                        link(dve.tensor_reduce(route_out[:, t, 1 + q, :].rearrange("p (h k) -> p h k", k=PEER_K), eq, AX.X, ALU.add))
                        yield

            def finish_choice():
                dve.wait_ge(gate_exp, blk)
                link(dve.tensor_reduce(ch_s[:, :, 0:8], ch_e, AX.X, ALU.add))
                link(dve.reciprocal(ch_s[:, :, 8:16], ch_s[:, :, 0:8]))
                dve.tensor_tensor(route_out[:, :, 0, :].rearrange("p t (h k) -> p t h k", k=PEER_K), ch_e,
                                  ch_s[:, :, 8:16].unsqueeze(3).broadcast_to([P, QT, PEER_HEADS, PEER_K]), ALU.mult).then_inc(route_done, 1)

            stage(f"u{blk}", steps_between=choose(), between={SLOTS_TILE: finish_choice}, begun=False)
            dve.wait_ge(slots_ready, 2 * blk)
            h0 = 64 * (blk - 1)

            def hot(g, half, wait):
                if wait:
                    dve.wait_ge(hot_used, g + (h0 - 1))
                four = [P, 4, P]
                dve.tensor_tensor(onehot[:, 0, 4 * half:4 * half + 4, :], iota.unsqueeze(1).broadcast_to(four),
                                  slots[:, 1, bass.ds(g * 4, 4)].unsqueeze(2).broadcast_to(four), ALU.is_equal)
                for j in range(4):
                    col, w = (slots[:, n, bass.ds(g * 4 + j, 1)] for n in (2, 0))
                    ins = dve.tensor_scalar(onehot[:, 1, 4 * half + j, :], iota, col, w, ALU.is_equal, ALU.mult)
                ins.then_inc(hot_ready, 1)

            if blk == 1:
                hot(0, 0, False)
                hot(1, 1, False)
            tiles(dve, 2 if blk == 1 else 0, 64, lambda g, u: hot(g, u, True))
            b = base[f"v{blk}"]

            def lows(i, u):
                dve.wait_ge(c_hi, i + (128 * (blk - 1) + 1))
                dve.tensor_tensor(act_hl[:, u, T:2 * T], gate_e[:, i, :], act_hl[:, u, 0:T].bitcast(F32), ALU.subtract).then_inc(c_lo, 1)
                low(i + b, (b + u) % 2)

            first = 0
            if blk == 1:
                tiles(dve, 0, 106, lows)
                first = 106
                for _ in dve_s5_inputs(dve, link):
                    lows(first, first % 2)
                    first += 1
            tiles(dve, first, 128, lambda i, u: lows(i, (first + u) % 2))
            dve.wait_ge(quarter_used, 4 * (b + 128))
            dve.wait_ge(x_again, 32 * blk)

            def add_experts(some):
                x2 = x_t[:, some].rearrange("p k t -> p (k t)")
                link(dve.tensor_tensor(x2, psum[:, some.start // 2:some.stop // 2, :].rearrange("p b n -> p (b n)"), x2, ALU.add))

            return add_experts

        def tv(n, k=1):
            return tiny[:, 8 * n:8 * (n + k)]

        g_row = tv(0, 2).rearrange("p (c g) -> p c g", c=QT)
        g_li, g_f = g_row[:, :, 0:4], g_row[:, :, 4:8]
        as_ch = lambda v: v.rearrange("p (c h) -> p c h", c=QT)
        soft, lf, cum, total, b_v = tv(2), tv(3), tv(4), tv(5), tv(6)
        d_max, m_int, m_t, neg_m = tv(7), tv(8), tv(9), tv(10)
        e_in = tv(11, 3)
        e_out = tv(14, 3)
        b_max, m_loc, m_new, w_k = tv(17)[:, 0:4], tv(17)[:, 4:8], tv(18)[:, 0:4], tv(18)[:, 4:8]
        den, r_den, ssq, ms, rt = tv(19), tv(20), tv(21), tv(22), tv(23)
        s_int = tv(24)
        cum_both = tv(4, 2)

        def pe_mlstm(pe):
            pe.wait_ge(tile_out, evac["out2"])
            for m in range(8):
                if m >= 2:
                    pe.wait_ge(vt_out, m - 1)
                for c in range(QT):
                    mm = pe.transpose(psum[:, 2 + m % 2, c * P:c * P + P], z_v[:, m, c * P:c * P + P], ident)
                mm.then_inc(vt_done, 1)
            pe.wait_ge(gate_bias, 1)
            for c in range(QT):
                mm = pe.transpose(psum[:, 4, c * P:c * P + P], z_g[:, 0, c * P:c * P + P], ident)
            mm.then_inc(gt_done, 1)
            pe.wait_ge(masks_loaded, 16)
            pe.wait_ge(lf_ready, 1)
            pe.matmul(psum[:, 5, 0:8], tri, lf, start=True, stop=True)
            pe.matmul(psum[:, 5, 8:16], ones, lf, start=True, stop=True).then_inc(cum_done, 1)
            pe.wait_ge(diag_ready, 1)
            for c in range(QT):
                for h in range(4):
                    mm = pe.matmul(psum[:, 6 + c, h * P:h * P + P], ones, diag[:, 4 * c + h, :], start=True, stop=True)
                mm.then_inc(row_done, 1)
            pe.wait_ge(qk_ready, 1)
            for m in range(8):
                mm = pe.transpose(psum[:, 4 + m // 4, (m % 4) * P:(m % 4) * P + P], qk[:, 8 + m, 0:P], ident)
            mm.then_inc(kt_done, 1)
            pe.wait_ge(kw_ready, 1)
            pe.wait_ge(vt_out, 8)
            for g in range(8):
                if g >= 2:
                    pe.wait_ge(st_out, g - 1)
                pe.matmul(psum[:, 2 + g % 2, 0:257], k_w[:, g * P:g * P + P], v_one[:, 0, g // 2, :],
                          start=True, stop=True).then_inc(st_done, 1)
            pe.wait_ge(decay_ready, 1)
            pe.wait_ge(kw_ready, 1)

            def scores2(u):
                c, h = divmod(u, 4)
                if u >= 2:
                    pe.wait_ge(pm_ready, u - 1)
                for d in range(2):
                    mm = pe.matmul(psum[:, 4 + u % 2, 0:P], qk[:, 2 * h + d, c * P:c * P + P], qk[:, 8 + 2 * h + d, c * P:c * P + P],
                                   start=d == 0, stop=d == 1)
                mm.then_inc(qk_done, 1)

            scores2(0)
            for u in range(8):
                c, h = divmod(u, 4)
                if u < 7:
                    scores2(u + 1)
                pe.wait_ge(pm_ready, u + 1)
                if u >= 2:
                    pe.wait_ge(pmt_ready, u - 1)
                pe.transpose(psum[:, 6 + u % 2, 0:P], p_m[:, u % 2, :], ident).then_inc(pmt_done, 1)
                pe.wait_ge(pmt_ready, u + 1)
                if u == 0:
                    pe.wait_ge(st_out, 8)
                if u >= 2:
                    pe.wait_ge(num_out, u - 1)
                pe.matmul(psum[:, 2 + u % 2, 0:257], pt_m[:, u % 2, :], v_one[:, c, h, :], start=True, stop=True).then_inc(num_done, 1)
                if c == 1:
                    if h >= 2:
                        pe.wait_ge(inter_out, h - 1)
                    for d in range(2):
                        mm = pe.matmul(psum[:, h % 2, 0:257], qk[:, 2 * h + d, P:2 * P], state[:, 2 * h + d, :], start=d == 0, stop=d == 1)
                    mm.then_inc(inter_done, 1)
            pe.wait_ge(hm_ready, 1)
            for k in range(8):
                if k >= 2:
                    pe.wait_ge(hmt_out, k - 1)
                for c in range(QT):
                    mm = pe.transpose(psum[:, 4 + k % 2, c * P:c * P + P], nums[:, 4 * c + k // 2, (k % 2) * P:(k % 2) * P + P], ident)
                mm.then_inc(hmt_done, 1)

        def act_mlstm(act):
            for m in range(8):
                act.wait_ge(vt_done, m + 1)
                act.copy(v_one[:, :, m // 2, (m % 2) * P:(m % 2) * P + P],
                         psum[:, 2 + m % 2, 0:T].rearrange("p (c n) -> p c n", c=QT)).then_inc(vt_out, 1)
            act.wait_ge(tile_out, evac["out2"])
            act.activation(z_o, z_o, ACT.Sigmoid).then_inc(o_gate_ready, 1)
            act.wait_ge(ml_in, 1)
            act.activation(soft, soft, ACT.Exp, scale=-1.0).then_inc(ml_out, 1)
            act.wait_ge(ml_in, 2)
            act.activation(soft, soft, ACT.Ln).then_inc(ml_out, 1)
            act.wait_ge(ml_in, 3)
            act.activation(e_out, e_in, ACT.Exp).then_inc(ml_out, 1)
            act.wait_ge(decay_in, 1)
            for u in range(8):
                ins = act.activation(decay[:, u, :], decay[:, u, :], ACT.Exp, bias=neg_m[:, u:u + 1])
            ins.then_inc(decay_ready, 1)
            for g in range(8):
                act.wait_ge(st_done, g + 1)
                act.copy(state[:, g, :], psum[:, 2 + g % 2, 0:257]).then_inc(st_out, 1)
            for u in range(8):
                act.wait_ge(pmt_done, u + 1)
                if u >= 2:
                    act.wait_ge(num_done, u - 1)
                act.copy(pt_m[:, u % 2, :], psum[:, 6 + u % 2, 0:P]).then_inc(pmt_ready, 1)
                act.wait_ge(num_done, u + 1)
                act.copy(nums[:, u, :], psum[:, 2 + u % 2, 0:257]).then_inc(num_out, 1)
            act.wait_ge(ml_in, 4)
            act.activation(rt, ms, ACT.Sqrt).then_inc(ml_out, 1)

        def dve_mlstm(dve, link):
            dve.wait_ge(tile_out, evac["out2"])
            dve.memset(v_one[:, :, :, 256:257], 1.0)
            dve.tensor_scalar(z_g[:, 0, :], z_g[:, 0, :], c_bias, None, ALU.add).then_inc(gate_bias, 1)
            dve.wait_ge(gt_done, 1)
            link(dve.tensor_copy(g_row, psum[:, 4, 0:T].rearrange("p (c n) -> p c n", c=QT)[:, :, 0:8]))
            dve.scalar_tensor_tensor(as_ch(soft), g_f, -1.0, g_f, ALU.mult, ALU.max).then_inc(ml_in, 1)
            dve.wait_ge(ml_out, 1)
            dve.tensor_scalar(soft, soft, 1.0, None, ALU.add).then_inc(ml_in, 1)
            dve.wait_ge(ml_out, 2)
            dve.scalar_tensor_tensor(as_ch(lf), g_f, 0.0, as_ch(soft), ALU.min, ALU.subtract).then_inc(lf_ready, 1)
            dve.wait_ge(cum_done, 1)
            link(dve.tensor_copy(cum_both, psum[:, 5, 0:16]))
            link(dve.tensor_tensor(as_ch(b_v), g_li, as_ch(cum), ALU.subtract))
            for u in range(8):
                ins = dve.tensor_scalar(diag[:, u, :], ident, b_v[:, u:u + 1], None, ALU.mult)
            ins.then_inc(diag_ready, 1)
            dve.wait_ge(row_done, 2)
            for u in range(8):
                ins = dve.scalar_tensor_tensor(decay[:, u, :], psum[:, 6 + u // 4, (u % 4) * P:(u % 4) * P + P], cum[:, u:u + 1], causal,
                                               ALU.add, ALU.add)
            link(dve.tensor_reduce(b_max, psum[:, 6, :].rearrange("p (h n) -> p h n", n=P), AX.X, ALU.max))
            dve.tensor_reduce(d_max, decay, AX.X, ALU.max)
            link(dve.tensor_tensor(m_loc, total[:, 0:4], b_max, ALU.add))
            link(dve.tensor_tensor(m_new, total[:, 0:4], m_loc, ALU.max))
            dve.tensor_copy(m_int[:, 0:4], cum[:, 0:4])
            link(dve.tensor_tensor(m_int[:, 4:8], cum[:, 4:8], m_new, ALU.add))
            link(dve.tensor_tensor(m_t, m_int, d_max, ALU.max))
            dve.tensor_scalar(neg_m, m_t, -1.0, None, ALU.mult).then_inc(decay_in, 1)
            dve.tensor_tensor(e_in[:, 0:8], m_int, m_t, ALU.subtract)
            dve.tensor_scalar(e_in[:, 8:16], m_t, -1.0, None, ALU.mult)
            dve.tensor_tensor(e_in[:, 16:20], b_v[:, 0:4], b_max, ALU.subtract)
            dve.tensor_tensor(e_in[:, 20:24], m_loc, m_new, ALU.subtract).then_inc(ml_in, 1)
            dve.wait_ge(ml_out, 3)
            scale = MLSTM_DIM ** -0.5
            dve.tensor_scalar(s_int, e_out[:, 0:8], scale, None, ALU.mult)
            link(dve.tensor_tensor(w_k, e_out[:, 16:20], e_out[:, 20:24], ALU.mult))
            dve.wait_ge(kt_done, 1)
            for h in range(4):
                ins = dve.tensor_scalar(k_w[:, 256 * h:256 * h + 256], psum[:, 4 + h // 2, (h % 2) * T:(h % 2) * T + T], w_k[:, h:h + 1],
                                        None, ALU.mult)
            ins.then_inc(kw_ready, 1)
            dve.wait_ge(decay_ready, 1)

            def add_inter(h):
                dve.wait_ge(inter_done, h + 1)
                dve.wait_ge(num_out, 5 + h)
                return dve.scalar_tensor_tensor(nums[:, 4 + h, :], psum[:, h % 2, 0:257], s_int[:, 4 + h:5 + h], nums[:, 4 + h, :],
                                                ALU.mult, ALU.add).then_inc(inter_out, 1)

            for u in range(8):
                dve.wait_ge(qk_done, u + 1)
                if u >= 2:
                    dve.wait_ge(pmt_done, u - 1)
                dve.scalar_tensor_tensor(p_m[:, u % 2, :], psum[:, 4 + u % 2, 0:P], scale, decay[:, u, :], ALU.mult, ALU.mult).then_inc(pm_ready, 1)
                if u >= 6:
                    add_inter(u - 6)
            add_inter(2)
            add_inter(3)
            dve.wait_ge(inter_out, 4)
            total_den = nums[:, :, 256]
            link(dve.scalar_tensor_tensor(den, total_den, -1.0, total_den, ALU.mult, ALU.max))
            link(dve.tensor_tensor(den, den, e_out[:, 8:16], ALU.max))
            link(dve.reciprocal(r_den, den))
            n256 = nums[:, :, 0:256]
            link(dve.tensor_tensor(n256, n256, r_den.unsqueeze(2).broadcast_to([P, 8, 256]), ALU.mult))
            sq = nums_sq.rearrange("p (u n) -> p u n", u=8)
            link(dve.tensor_tensor(sq, n256, n256, ALU.mult))
            link(dve.tensor_reduce(ssq, sq, AX.X, ALU.add))
            dve.tensor_scalar(ms, ssq, 1.0 / MLSTM_DIM, EPS, ALU.mult, ALU.add).then_inc(ml_in, 1)
            dve.wait_ge(ml_out, 4)
            link(dve.reciprocal(r_den, rt))
            dve.tensor_tensor(n256, n256, r_den.unsqueeze(2).broadcast_to([P, 8, 256]), ALU.mult).then_inc(hm_ready, 1)
            dve.wait_ge(o_gate_ready, 1)
            for k in range(8):
                dve.wait_ge(hmt_done, k + 1)
                dve.scalar_tensor_tensor(mix[:, k, :], psum[:, 4 + k % 2, 0:T], c_mlstm[:, k:k + 1], z_o[:, k, :], ALU.mult, ALU.mult).then_inc(hmt_out, 1)

        def pe_s5_inputs(pe):
            for part in range(2):
                pe.wait_ge(blk_ready, part + 1)
                for half in range(2):
                    for j in range(4):
                        k = 4 * half + j
                        mm = pe.transpose(psum[:, 3 + 2 * part + half, j * P:j * P + P], b_blk[part][:, k * P:k * P + P], ident)
                    mm.then_inc(bt_done, 1)

        def pe_s5(pe):
            pe.wait_ge(bt_out, 4)
            pe.wait_ge(blk_ready, 5)

            def drive(g):
                j, i = divmod(g, 4)
                pe.wait_ge(tile_out, evac["z2"] + j + 1)
                if g >= 2:
                    pe.wait_ge(xs_used, g - 1)
                for part in range(2):
                    mm = pe.matmul(psum[:, 2 + g % 2, part * T:part * T + T], b_in[part][32 * i:32 * i + 32, j, :],
                                   z_u[32 * i:32 * i + 32, j, :], start=True, stop=True)
                mm.then_inc(xs_done, 1)

            def outputs(g):
                j, i = divmod(g, 4)
                pe.wait_ge(ys_in, g + 1)
                if i == 0 and j >= 2:
                    pe.wait_ge(ys_out, j - 1)
                out = psum[32 * i:32 * i + 32, 4 + j % 2, 0:T]
                b = 2 * (g % 2)
                terms = [(0, y_cos[:, b, :]), (1, y_sin[:, b + 1, :]), (2, y_sin[:, b, :]), (2, y_cos[:, b + 1, :])]
                for n, (m, rhs) in enumerate(terms):
                    mm = pe.matmul(out, c_blk[m][:, 32 * g:32 * g + 32], rhs, start=n == 0, stop=n == 3)
                mm.then_inc(ys_done, 1)

            for step in range(36):
                for g in in_step(step, 2, S5_TILES):
                    drive(g)
                for g in in_step(step, 4, S5_TILES):
                    outputs(g)
                yield

        def pe_glu(pe):
            pe.wait_ge(glu_ready, 1)
            for j in range(8):
                pe.wait_ge(y_gelu, 1)
                if j >= 2:
                    pe.wait_ge(glu_out, j - 1)
                for part in range(2):
                    mm = pe.matmul(psum[:, 6 + j % 2, part * T:part * T + T], glu_w[part][:, j, :], y_g[:, j, :], start=True, stop=True)
                mm.then_inc(glu_done, 1)

        def act_s5_loads(act):
            act.wait_ge(c_lo, 100)
            act.dma_start(s5v[:, 0:3, :], a["lam"]).then_inc(s5_loaded, 16)
            for n, (dst, name) in enumerate(zip(b_raw + c_raw, ("b_re", "b_im", "c_re", "c_im"))):
                act.dma_start(dst, a[name]).then_inc(s5_loaded, 16)

        def act_s5_decay(act):
            act.wait_ge(s5_loaded, 80)
            act.activation(s5v[:, 3, :], s5v[:, 2, :], ACT.Exp).then_inc(s5_out, 1)
            act.wait_ge(s5_in, 1)
            act.activation(s5v[:, 4, :], s5v[:, 4, :], ACT.Exp).then_inc(s5_out, 1)

        def act_s5_turn(act):
            act.wait_ge(s5_in, 2)
            act.activation(s5v[:, 6:8, :], s5v[:, 6:8, :], ACT.Sin).then_inc(s5_out, 1)

        def act_s5_inputs(act):
            for n in range(4):
                act.wait_ge(bt_done, n + 1)
                part, half = divmod(n, 2)
                act.copy(b_in[part][:, 4 * half:4 * half + 4, :].rearrange("p j s -> p (j s)"), psum[:, 3 + n, :]).then_inc(bt_out, 1)

        def act_s5(act):
            two_pi = 2 * math.pi * (1 - 2e-7)
            for step in range(1, 40):
                for j in range(8):
                    if step == 4 * j + 1:
                        act.wait_ge(table_in, j + 1)
                        if j >= 2:
                            act.wait_ge(ys_in, 4 * j - 4)
                        act.activation(sin_t[j % 2], near_t, ACT.Sin, scale=-two_pi)
                        act.activation(cos_t[j % 2], turn_t, ACT.Sin, scale=-two_pi, bias=c_half_pi).then_inc(table_ready, 1)
                if step == 37:
                    act.wait_ge(conv_done, 1)
                    act.activation(qk, qk, ACT.Silu).then_inc(qk_ready, 1)
                if step == 39:
                    act.wait_ge(ys_out, 8)
                    act.activation(y_g, y_g, ACT.Gelu).then_inc(y_gelu, 1)
                yield

        def act_glu(act):
            for j in range(8):
                act.wait_ge(glu_done, j + 1)
                if j >= 2:
                    act.wait_ge(glu_out, j - 1)
                act.activation(x_cos[:, j % 2, :], psum[:, 6 + j % 2, T:2 * T], ACT.Sigmoid).then_inc(glu_sig, 1)

        def dve_s5_inputs(dve, link):
            L = lambda n: s5v[:, n, :]
            lre, lim, dt, mag, th, sin, cos = L(0), L(1), L(3), L(4), L(5), L(6), L(7)
            ar1, ai, d2, fr, fi, t0 = L(8), L(9), L(10), L(11), L(12), L(13)
            dve.wait_ge(s5_out, 1)
            dve.tensor_tensor(th, lim, dt, ALU.mult)
            dve.tensor_tensor(mag, lre, dt, ALU.mult).then_inc(s5_in, 1)
            dve.wait_ge(s5_in, 1)
            yield
            reduce_angle(dve, link, th, t0)
            link(dve.tensor_copy(sin, th))
            link(dve.scalar_tensor_tensor(cos, th, -1.0, th, ALU.mult, ALU.max))
            dve.tensor_scalar(cos, cos, -1.0, math.pi / 2, ALU.mult, ALU.add).then_inc(s5_in, 1)
            yield
            yield
            dve.wait_ge(s5_out, 3)
            link(dve.tensor_tensor(ar1, mag, cos, ALU.mult))
            dve.tensor_scalar(ar1, ar1, 1.0, None, ALU.subtract)
            dve.tensor_tensor(ai, mag, sin, ALU.mult)
            dve.tensor_tensor(d2, lre, lre, ALU.mult)
            link(dve.tensor_tensor(t0, lim, lim, ALU.mult))
            link(dve.tensor_tensor(d2, d2, t0, ALU.add))
            link(dve.reciprocal(d2, d2))
            for out, x, y, op in ((fr, ar1, ai, ALU.add), (fi, ai, ar1, ALU.subtract)):
                dve.tensor_tensor(out, x, lre, ALU.mult)
                link(dve.tensor_tensor(t0, y, lim, ALU.mult))
                link(dve.tensor_tensor(out, out, t0, op))
                link(dve.tensor_tensor(out, out, d2, ALU.mult))
            yield
            link(dve.tensor_scalar(th, th, 1 / (2 * math.pi), None, ALU.mult))
            g16 = [P, S5_TILES, 16]
            wide = lambda v: v.unsqueeze(2).broadcast_to(g16)
            for out, x, y, op in ((b_bar[0], b_raw[0], b_raw[1], ALU.subtract), (b_bar[1], b_raw[1], b_raw[0], ALU.add)):
                dve.tensor_tensor(out, x, wide(fr), ALU.mult)
                link(dve.tensor_tensor(b_tmp, y, wide(fi), ALU.mult))
                link(dve.tensor_tensor(out, out, b_tmp, op))
                yield
            blk4 = [P, S5_TILES, 2, 16]
            pair = c_pair.unsqueeze(1).unsqueeze(3).broadcast_to(blk4)

            def to_blocks(dst, src):
                dve.tensor_tensor(dst.rearrange("p (g q h) -> p g q h", q=2, h=16), src.unsqueeze(2).broadcast_to(blk4), pair,
                                  ALU.mult).then_inc(blk_ready, 1)

            to_blocks(b_blk[0], b_bar[0])
            yield
            to_blocks(b_blk[1], b_bar[1])
            yield
            to_blocks(c_blk[0], c_raw[0])
            yield
            dve.wait_ge(blk_ready, 3)
            link(dve.tensor_scalar(c_raw[0], c_raw[0], -1.0, None, ALU.mult))
            to_blocks(c_blk[1], c_raw[0])
            yield
            link(dve.tensor_scalar(c_raw[1], c_raw[1], -1.0, None, ALU.mult))
            to_blocks(c_blk[2], c_raw[1])
            yield

        def dve_s5(dve, link):
            mag, th = s5v[:, 4, :], s5v[:, 5, :]

            def y_leave(j):
                dve.wait_ge(ys_done, 4 * j + 4)
                dve.scalar_tensor_tensor(y_g[:, j, :], z_u[:, j, :], c_d[:, j:j + 1], psum[:, 4 + j % 2, 0:T], ALU.mult, ALU.add).then_inc(ys_out, 1)

            magic = 12582912.0

            def turns(j):
                if j:
                    dve.wait_ge(table_ready, j)
                for k in range(4):
                    speed = th[:, 4 * j + k:4 * j + k + 1]
                    dve.tensor_scalar(turn_t[:, k, 0:P], iota, speed, None, ALU.mult)
                    ins = dve.tensor_scalar(turn_t[:, k, P:T], iota, float(P), speed, ALU.add, ALU.mult)
                link(ins)

            def near(_):
                link(dve.tensor_scalar(near_t, turn_t, magic, None, ALU.add))
                link(dve.scalar_tensor_tensor(near_t, near_t, magic, turn_t, ALU.subtract, ALU.subtract))
                dve.scalar_tensor_tensor(turn_t, near_t, -1.0, near_t, ALU.mult, ALU.max).then_inc(table_in, 1)

            def follow(g):
                j, i = divmod(g, 4)
                if i == 0:
                    dve.wait_ge(table_ready, j + 1)
                two = [P, 2, T]
                cs, sn = (t[j % 2][:, i, :].unsqueeze(1).broadcast_to(two) for t in (cos_t, sin_t))
                m = mag[:, g:g + 1].broadcast_to([P, T])
                dve.wait_ge(xs_done, g + 1)
                x = psum[:, 2 + g % 2, :].rearrange("p (q t) -> p q t", q=2)
                dve.tensor_tensor(x_cos, x, cs, ALU.mult)
                dve.tensor_tensor(x_sin, x, sn, ALU.mult).then_inc(xs_used, 1)
                dve.wait_ge(xs_used, g + 1)
                dve.tensor_tensor(x_rot[:, 0, :], x_cos[:, 0, :], x_sin[:, 1, :], ALU.add)
                link(dve.tensor_tensor(x_rot[:, 1, :], x_cos[:, 1, :], x_sin[:, 0, :], ALU.subtract))
                if g >= 2:
                    dve.wait_ge(ys_in, g - 1)
                b = 2 * (g % 2)
                dve.tensor_tensor_scan(s_rot[:, b, :], m, x_rot[:, 0, :], 0.0, ALU.mult, ALU.add)
                dve.tensor_tensor_scan(s_rot[:, b + 1, :], m, x_rot[:, 1, :], 0.0, ALU.mult, ALU.add).then_inc(s_ready, 1)
                dve.wait_ge(s_ready, g + 1)

            def convolve(k):
                if k == 0:
                    dve.wait_ge(x_kept, 32)
                dve.wait_ge(tile_out, evac["z2"] + 10 + k)
                for tap in (3, 2, 1, 0):
                    lag, w = 3 - tap, c_conv[:, k, tap:tap + 1]
                    if lag == 0:
                        ins = dve.tensor_scalar(qk[:, k, :], z_qk[:, k, :], w, None, ALU.mult)
                    else:
                        ins = dve.scalar_tensor_tensor(qk[:, k, lag:T], z_qk[:, k, 0:T - lag], w, qk[:, k, lag:T], ALU.mult, ALU.add)
                    if tap:
                        link(ins)
                if k == 15:
                    ins.then_inc(conv_done, 1)

            turns(0)
            near(0)
            for step in range(1, 39):
                if step > 1:
                    for g in in_step(step, 3, S5_TILES):
                        follow(g)
                        j, i = divmod(g, 4)
                        if i == 0 and j < 7:
                            turns(j + 1)
                        if i == 1 and j < 7:
                            near(j + 1)
                        if i == 2 and j >= 1:
                            y_leave(j - 1)
                    for k in in_step(step, 20, 16):
                        convolve(k)
                    for _ in in_step(step, 37, 1):
                        y_leave(7)
                yield

        def dve_glu(dve):
            eight = c_eight.unsqueeze(1).unsqueeze(3).broadcast_to([P, 8, 8, 16])
            dve.wait_ge(glu_loaded, 16)
            dve.wait_ge(ys_done, S5_TILES)
            for part in range(2):
                src = glu_raw[:, :, 16 * part:16 * part + 16].unsqueeze(2).broadcast_to([P, 8, 8, 16])
                ins = dve.tensor_tensor(glu_w[part].rearrange("p j (g k) -> p j g k", k=16), src, eight, ALU.mult)
            ins.then_inc(glu_ready, 1)
            for j in range(8):
                dve.wait_ge(glu_sig, j + 1)
                dve.tensor_tensor(mix[:, 8 + j, :], psum[:, 6 + j % 2, 0:T], x_cos[:, j % 2, :], ALU.mult).then_inc(glu_out, 1)

        @block.sync
        def _(sp):
            for c in range(4):
                sp.dma_start(x_t[:, 4 * c:4 * c + 4], a["x"][:, 4 * c:4 * c + 4]).then_inc(x_loaded[c], 16)

            def stream(stage, w, between={}):
                b = base[stage]

                def load(i, par, wait):
                    for h in range(2):
                        j = 2 * par + h
                        if wait:
                            sp.wait_ge(lo_ready, (i + b) * 4 + 2 * h - 6)
                        sp.dma_start(raw[:, j, :], w[i, h]).then_inc(raw_loaded[j], 16)

                first = 0
                if b == 0:
                    load(0, 0, False)
                    load(1, 1, False)
                    first = 2
                for stop in sorted(between) + [nstage[stage]]:
                    tiles(sp, first, stop, lambda i, u: load(i, bank_of(b, first, u), True))
                    if stop in between:
                        between[stop]()
                    first = stop

            def residual_back(blk):
                sp.wait_ge(c_lo, 128 * (blk - 1) + 16)
                sp.wait_ge(x_kept, {1: 16, 2: 48}[blk])
                sp.dma_start(x_t, x_mid).then_inc(x_again, 16)

            stream("proj1", a["w_proj1"])
            stream("gates1", a["w_gates1"])
            sp.wait_ge(o_ready, 16)
            sp.dma_start(x1, a["x"]).then_inc(x_again, 16)
            stream("branch1", a["w_branch1"])
            stream("out1", a["w_out1"])
            sp.wait_ge(tile_out, evac["wq1"])
            sp.dma_start(x_mid, x1).then_inc(x_kept, 16)
            stream("wq1", a["w_q1"])
            stream("u1", a["u1"])
            stream("v1", a["v1"], between={64: lambda: residual_back(1)})
            sp.wait_ge(block_in, 4)
            sp.dma_start(x_mid, xb).then_inc(x_kept, 16)
            stream("z2", a["w_z2"])
            sp.wait_ge(conv_done, 1)
            sp.wait_ge(glu_done, 8)
            sp.wait_ge(gt_done, 1)
            sp.wait_ge(x_kept, 32)
            sp.dma_start(x1, x_mid).then_inc(x_again, 16)
            stream("out2", a["w_out2"])
            sp.wait_ge(tile_out, evac["wq2"])
            sp.dma_start(x_mid, x1).then_inc(x_kept, 16)
            stream("wq2", a["w_q2"])
            stream("u2", a["u2"])
            stream("v2", a["v2"], between={64: lambda: residual_back(2)})
            for c in range(4):
                sp.wait_ge(block_in, 4 + c + 1)
                sp.dma_start(a["out"][:, 4 * c:4 * c + 4], xb[:, 4 * c:4 * c + 4]).then_inc(out_stored, 16)
            sp.wait_ge(out_stored, 64)

        @block.tensor
        def _(pe):
            def quarter(ps, c, start, stop):
                for kk in range(4):
                    k = 4 * c + kk
                    w_h, w_l = w_hi[:, c, kk * P:kk * P + P], w_lo[:, c, kk * P:kk * P + P]
                    pe.matmul(ps, w_h, act_hl[:, k, 0:T], start=start and kk == 0, stop=False)
                    pe.matmul(ps, w_h, act_hl[:, k, T:2 * T], start=False, stop=False)
                    mm = pe.matmul(ps, w_l, act_hl[:, k, 0:T], start=False, stop=stop and kk == 3)
                mm.then_inc(quarter_used, 1)

            def gemm(stage, halves=1, steps_between=(), between={}, acts=0):
                b, e = base[stage], evac[stage]

                def one(i, par, wait, chunks=0):
                    if wait:
                        pe.wait_ge(tile_out, i + (e - 1))
                    for c in range(4):
                        if chunks:
                            pe.wait_ge(act_ready, 4 * (chunks - 1) + c + 1)
                        pe.wait_ge(lo_ready, (i + b) * 4 + c + 1)
                        if halves == 1:
                            quarter(psum[:, par, 0:T], c, c == 0, c == 3)
                        else:
                            h = c // 2
                            quarter(psum[:, par, h * T:h * T + T], c, c % 2 == 0, c % 2 == 1)

                first = 0
                if e == 0:
                    one(0, 0, False, acts)
                    one(1, 1, False)
                    first = 2
                for _ in steps_between:
                    one(first, (b + first) % 2, True, 0 if first else acts)
                    first += 1
                if acts and first == 0:
                    one(0, b % 2, True, acts)
                    first = 1
                for stop in sorted(between) + [nstage[stage]]:
                    tiles(pe, first, stop, lambda i, u: one(i, bank_of(b, first, u), True))
                    if stop in between:
                        between[stop]()
                    first = stop

            def sum_squares(n, src, nt):
                if n == 0:
                    pe.wait_ge(consts_loaded, 32)
                for k in range(nt):
                    if k % 4 == 0:
                        pe.wait_ge(sq_ready, SQ_BASE[n] + (2 if k == 0 and n in (4, 7) else k // 4 + 1))
                    mm = pe.matmul(psum[:, 2, 0:T], ones, src[:, k, :], start=k == 0, stop=k == nt - 1)
                mm.then_inc(sum_ready, 1)

            sum_squares(0, tmp, 16)
            gemm("proj1", acts=1)

            pe.wait_ge(tile_out, evac["gates1"])
            sum_squares(1, low_sq[:, 0:4, :], 4)
            sum_squares(2, low_sq[:, 4:6, :], 2)
            pe.wait_ge(norm_ready, 1)
            pe.wait_ge(small_loaded, 48)
            for m in range(8 + 4 + 8 + 4):
                bank = 3 + m % 2
                if m >= 2:
                    pe.wait_ge(up_out, m - 1)
                ps = psum[:, bank, 0:T]
                if m == 12:
                    pe.wait_ge(norm_ready, 2)
                if m < 8:
                    ops = [(w_uq[:, k, P * m:P * m + P], proj[:, CQ + k, :]) for k in range(4)]
                elif m < 12:
                    ops = [(w_uq[:, k, P * m:P * m + P], proj[:, CQ + k, :]) for k in range(4)]
                elif m < 20:
                    h = m - 12
                    ops = [(w_uk[:, k, P * h:P * h + P], proj[:, CKV + k, :]) for k in range(2)]
                else:
                    t, n = divmod(m - 20, 2)
                    ps = psum[:, bank, :]
                    ops = [(proj[:, CKV + k, t * P:t * P + P], w_uv[:, k, n * 512:n * 512 + 512]) for k in range(2)]
                for j, (lhs, rhs) in enumerate(ops):
                    mm = pe.matmul(ps, lhs, rhs, start=j == 0, stop=j == len(ops) - 1)
                mm.then_inc(up_done, 1)

            for t in range(QT):
                if t == 1:
                    pe.wait_ge(turn_out, 1)
                for g in range(2):
                    pe.transpose(psum[:, 7, g * P:g * P + P], proj[:, DV + g, t * P:t * P + P], ident)
                pe.transpose(psum[:, 7, 2 * P:3 * P], proj[:, IW, t * P:t * P + P], ident).then_inc(turn_done, 1)

            def rotate(j):
                x, kind = rots[j]
                bank = 2 + j if j < 6 else 6 + j % 2
                if j == 5:
                    pe.wait_ge(turn_out, 2)
                if j >= 6:
                    pe.wait_ge(rot_used, 6 if j < 8 else j - 1)
                if isinstance(x, int):
                    pe.matmul(psum[:, bank, 0:T], mats[:, 3 + 2 * x, :], proj[:, KI, :], start=True, stop=True)
                    mm = pe.matmul(psum[:, bank, T:2 * T], mats[:, 4 + 2 * x, :], proj[:, KI, :], start=True, stop=True)
                else:
                    mm = pe.matmul(psum[:, bank, :], mats[:, kind, :], x, start=True, stop=True)
                mm.then_inc(rot_done, 1)

            def dots(batch):
                t, h0 = batch // 2, 8 * (batch % 2)
                pe.wait_ge(rot_used, N_IDX_ROT)
                if batch >= 2:
                    pe.wait_ge(relu_done, batch)
                for n in range(8):
                    h = h0 + n
                    bank, at = (2 + 2 * batch + n // 4, (n % 4) * P) if t == 0 else (2 + n // 2, (n % 2) * T)
                    mm = pe.matmul(psum[:, bank, at:at + P * (t + 1)], proj[:, IQ + h // 2, t * P:t * P + P],
                                   ik[:, h % 2, 0:P * (t + 1)], start=True, stop=True)
                mm.then_inc(dots_done, 1)

            def scores(p):
                br, h = divmod(p, 8)
                pe.wait_ge(rot_used, N_ROT if br else N_MLA_ROT)
                pe.wait_ge(relu_done, 4)
                if p >= 2:
                    pe.wait_ge(s_shifted, p - 1)
                for t in range(QT):
                    nk = P * (t + 1)
                    ps = psum[:, 2 + p % 2, P * t:P * t + nk]
                    if br == 0:
                        pe.matmul(ps, q_nope[:, h, t * P:t * P + P], k_nope[:, h, 0:nk], start=True, stop=False)
                        mm = pe.matmul(ps, q_rope[:, h // 2, t * P:t * P + P], k_pe[:, h % 2, 0:nk], start=False, stop=True)
                    else:
                        mm = pe.matmul(ps, proj[:, DQ + h, t * P:t * P + P], proj[:, DK + h // 4, 0:nk], start=True, stop=True)
                mm.then_inc(s_done, 1)

            def turn_probs(p):
                pe.wait_ge(p_ready, p + 1)
                if p >= 2:
                    pe.wait_ge(pt_ready, p - 1)
                for k in range(3):
                    mm = pe.transpose(psum[:, 4 + p % 2, k * P:k * P + P], s_sb[:, p % 3, k * P:k * P + P], ident)
                mm.then_inc(pt_done, 1)

            def values(p):
                br, h = divmod(p, 8)
                pe.wait_ge(pt_ready, p + 1)
                if p >= 2:
                    pe.wait_ge(o_ready, p - 1)
                for t in range(QT):
                    for kt in range(t + 1):
                        v = v_row[:, kt, h * P:h * P + P] if br == 0 else dv_row[:, kt, (h // 4) * P:(h // 4) * P + P]
                        at = (t + kt) * P
                        mm = pe.matmul(psum[:, 6 + p % 2, t * P:t * P + P], v, p_t[:, p % 2, at:at + P], start=kt == 0, stop=kt == t)
                mm.then_inc(o_done, 1)

            def attend():
                pe.wait_ge(consts_loaded, 64)
                pe.wait_ge(up_out, 24)
                for step in range(ATTENTION_STEPS):
                    for j in rots_of(step):
                        rotate(j)
                    for batch in in_step(step, 4, 4):
                        dots(batch)
                    for p in in_step(step, 9, 16):
                        scores(p)
                    for p in in_step(step, 12, 16):
                        turn_probs(p)
                    for p in in_step(step, 14, 16):
                        values(p)
                    yield

            gemm("gates1", steps_between=attend())
            gemm("branch1", halves=2, acts=2)
            gemm("out1", acts=3)
            experts(pe, 1, sum_squares, gemm, quarter)
            sum_squares(4, tmp, 16)
            pe_s5_inputs(pe)
            sum_squares(5, tmp, 16)
            gemm("z2", steps_between=pe_s5(pe), acts=5)
            pe_glu(pe)
            pe_mlstm(pe)
            gemm("out2", acts=6)
            experts(pe, 2, sum_squares, gemm, quarter)
            sum_squares(7, tmp, 16)

        @block.scalar
        def _(act):
            act.dma_start(pos_i[:, 0, :].bitcast(I32), a["positions"].partition_broadcast(P)).then_inc(pos_loaded, 16)
            act.dma_start(consts[:, :, :], a["consts"]).then_inc(consts_loaded, 16)
            act.dma_start(cols[:, :], a["cols"]).then_inc(consts_loaded, 16)
            act.dma_start(w_uq, a["w_uq"]).then_inc(small_loaded, 16)
            act.dma_start(w_uk, a["w_uk"]).then_inc(small_loaded, 16)
            act.dma_start(w_uv, a["w_uv"]).then_inc(small_loaded, 16)

            def root(n):
                act.wait_ge(mean_ready, n + 1)
                act.activation(stat[:, 1, :], stat[:, 0, :], ACT.Sqrt).then_inc(root_ready, 1)

            def split(T0, par, wait):
                for c in range(4):
                    if c % 2 == 0:
                        j = 2 * par + c // 2
                        act.wait_ge(raw_loaded[j], (T0 - par) * 8 + 16)
                    if wait:
                        act.wait_ge(quarter_used, T0 * 4 + c - 3)
                    act.copy(w_hi[:, c, :], raw[:, 2 * par + c // 2, (c % 2) * 512:(c % 2) * 512 + 512]).then_inc(hi_ready, 1)

            def begin(name):
                split(base[name], base[name] % 2, base[name] > 0)

            def stage(name, leave=None, steps_between=(), between={}, begun=False):
                b, n = base[name], nstage[name]
                if not begun:
                    begin(name)

                def body(i, par):
                    split(i + b, par, True)
                    if leave:
                        leave(i - 1, 1 - par)

                first = 1
                for _ in steps_between:
                    body(first, (b + first) % 2)
                    first += 1
                for stop in sorted(between) + [n]:
                    tiles(act, first, stop, lambda i, u: body(i, bank_of(b, first, u)))
                    if stop in between:
                        between[stop]()
                    first = stop
                if leave:
                    leave(n - 1, (b + n - 1) % 2)

            def plain(name, dst):
                b = base[name]

                def leave(i, par):
                    act.wait_ge(quarter_used, (i + b) * 4 + 4)
                    act.copy(dst[:, i, :], psum[:, par, 0:T]).then_inc(tile_out, 1)
                return leave

            act.wait_ge(angle_ready, 2)
            act.activation(rope_s, rope_s, ACT.Sin)
            act.activation(rope_c, rope_c, ACT.Sin).then_inc(sin_ready, 1)
            begin("proj1")
            root(0)
            act.wait_ge(act_ready, 4)
            act.dma_start(mats, a["mats"]).then_inc(consts_loaded, 16)
            act.dma_start(mask, a["mask"]).then_inc(consts_loaded, 16)
            stage("proj1", plain("proj1", proj), begun=True)
            root(1)
            root(2)
            for m in range(24):
                act.wait_ge(up_done, m + 1)
                bank = 3 + m % 2
                if m < 8:
                    act.copy(q_nope[:, m, :], psum[:, bank, 0:T]).then_inc(up_out, 1)
                elif m < 12:
                    act.copy(q_rope[:, m - 8, :], psum[:, bank, 0:T]).then_inc(up_out, 1)
                elif m < 20:
                    act.copy(k_nope[:, m - 12, :], psum[:, bank, 0:T]).then_inc(up_out, 1)
                else:
                    t, n = divmod(m - 20, 2)
                    act.copy(v_row[:, t, n * 512:n * 512 + 512], psum[:, bank, :]).then_inc(up_out, 1)
            for t in range(QT):
                act.wait_ge(turn_done, t + 1)
                act.copy(dv_row[:, t, :], psum[:, 7, 0:T])
                act.mul(iw_row[:, t, :], psum[:, 7, 2 * P:2 * P + IDX_HEADS], IDX_HEADS ** -0.5).then_inc(turn_out, 1)

            def relus(batch):
                t = batch // 2
                act.wait_ge(dots_done, batch + 1)
                if batch:
                    act.wait_ge(dots_used, batch)
                lo, n = (2 + 2 * batch, 2) if t == 0 else (2, 4)
                act.activation(relu[:, 0:512 * n], psum[:, lo:lo + n, :].rearrange("p b n -> p (b n)"), ACT.Relu,
                               scale=IDX_DIM ** -0.5).then_inc(relu_done, 1)

            def exponentials1(p):
                act.wait_ge(s_shifted, p + 1)
                for t in range(QT):
                    s = s_sb[:, p % 3, P * t:P * t + P * (t + 1)]
                    ins = act.activation(s, s, ACT.Exp, bias=soft_c[:, p % 2, 0, t:t + 1], accum_out=soft_c[:, p % 2, 1, t:t + 1])
                ins.then_inc(p_exp, 1)

            def probs_leave(p):
                act.wait_ge(pt_done, p + 1)
                act.wait_ge(dots_used, 4)
                if p >= 2:
                    act.wait_ge(o_done, p - 1)
                act.copy(p_t[:, p % 2, :], psum[:, 4 + p % 2, 0:3 * P]).then_inc(pt_ready, 1)

            def values_leave(p):
                act.wait_ge(o_done, p + 1)
                act.copy(o_heads[:, p, :], psum[:, 6 + p % 2, 0:T]).then_inc(o_ready, 1)

            def attend():
                for step in range(1, ATTENTION_STEPS):
                    for p in in_step(step, 15, 16):
                        values_leave(p)
                    for p in in_step(step, 13, 16):
                        probs_leave(p)
                    for batch in in_step(step, 5, 4):
                        relus(batch)
                    for p in in_step(step, 10, 16):
                        exponentials1(p)
                    yield

            def gate_leave(i, par):
                act.wait_ge(quarter_used, (i + base["gates1"]) * 4 + 4)
                act.copy(gates[i // 16][:, i % 16, :], psum[:, par, 0:T]).then_inc(tile_out, 1)

            stage("gates1", gate_leave, steps_between=attend())
            act.wait_ge(tile_out, evac["branch1"])
            for g in gates:
                act.activation(g, g, ACT.Sigmoid).then_inc(gates_ready, 1)
            stage("branch1")
            stage("out1")
            act_experts(act, 1, root, begin, stage, plain, split)
            root(4)
            act.dma_start(flat(127, 128), a["tri"]).then_inc(masks_loaded, 16)
            act.dma_start(glu_raw, a["glu"]).then_inc(glu_loaded, 16)
            act_s5_inputs(act)
            begin("z2")
            root(5)
            stage("z2", plain("z2", z), steps_between=act_s5(act), begun=True)
            act_glu(act)
            act_mlstm(act)
            stage("out2")
            act_experts(act, 2, root, begin, stage, plain, split)
            root(7)

        @block.gpsimd
        def _(pool):
            for blk in range(2):
                pool.wait_ge(tile_out, evac[f"u{blk + 1}"] + 128)

                def weigh(g, half):
                    pool.wait_ge(gate_out, g + (128 * blk + 1))
                    e = gate_e[:, :, bass.ds(g * 2, 2)]
                    pool.tensor_tensor(e, gate_tmp[:, half], e, ALU.mult).then_inc(weighed, 1)

                tiles(pool, 0, 128, weigh)
                if blk == 0:
                    for g in range(S5_TILES):
                        j, i = divmod(g, 4)
                        cs, sn = (t[j % 2][:, i, :].unsqueeze(1).broadcast_to([P, 2, T]) for t in (cos_t, sin_t))
                        pool.wait_ge(s_ready, g + 1)
                        if g >= 2:
                            pool.wait_ge(ys_done, g - 1)
                        b = 2 * (g % 2)
                        pool.tensor_tensor(y_cos[:, b:b + 2, :], s_rot[:, b:b + 2, :], cs, ALU.mult)
                        pool.tensor_tensor(y_sin[:, b:b + 2, :], s_rot[:, b:b + 2, :], sn, ALU.mult).then_inc(ys_in, 1)

        @block.vector
        def _(dve):
            steps = [0]

            def link(ins):
                steps[0] += 1
                ins.then_inc(dve_step, 1)
                dve.wait_ge(dve_step, steps[0])

            def rms(n, src, nt, dim, gain, dst, scr, begun=None, before=None):
                for lo in range(0, nt, 4):
                    some = slice(lo, min(lo + 4, nt))
                    if n == 0:
                        dve.wait_ge(x_loaded[lo // 4], 16)
                    if before:
                        before(some)
                    dve.tensor_tensor(scr[:, some], src[:, some], src[:, some], ALU.mult).then_inc(sq_ready, 1)
                dve.wait_ge(sq_ready, SQ_BASE[n] + -(-nt // 4))
                link(dve.tensor_tensor(dst, src, gain.unsqueeze(2).broadcast_to([P, nt, T]), ALU.mult))
                if begun:
                    low(base[begun], base[begun] % 2)
                dve.wait_ge(sum_ready, n + 1)
                dve.tensor_scalar(stat[:, 0, :], psum[:, 2, 0:T], 1.0 / dim, EPS, ALU.mult, ALU.add).then_inc(mean_ready, 1)
                dve.wait_ge(root_ready, n + 1)
                link(dve.reciprocal(stat[:, 2, :], stat[:, 1, :]))

            def scaled(dst):
                return dve.tensor_tensor(dst, dst, stat[:, 2, :].unsqueeze(1).broadcast_to([P, dst.shape[1], T]), ALU.mult)

            def split_act(src, used, norm=False, begun=None):
                if used:
                    dve.wait_ge(quarter_used, used)
                for c in range(4):
                    some = slice(4 * c, 4 * c + 4)
                    if norm:
                        link(scaled(src[:, some]))
                    link(dve.tensor_copy(act_hl[:, some, 0:T], src[:, some]))
                    dve.tensor_tensor(act_hl[:, some, T:2 * T], src[:, some], act_hl[:, some, 0:T].bitcast(F32), ALU.subtract).then_inc(act_ready, 1)
                    if begun and c == 0:
                        low(base[begun], base[begun] % 2)

            def low(T0, par):
                for c in range(4):
                    dve.wait_ge(hi_ready, T0 * 4 + (c + 1))
                    dve.tensor_tensor(w_lo[:, c, :], raw[:, 2 * par + c // 2, (c % 2) * 512:(c % 2) * 512 + 512],
                                      w_hi[:, c, :].bitcast(F32), ALU.subtract).then_inc(lo_ready, 1)

            def stage(name, leave=None, steps_between=(), between={}, begun=True):
                b, n = base[name], nstage[name]
                if not begun:
                    low(b, b % 2)

                def body(i, par):
                    low(i + b, par)
                    if leave:
                        leave(i - 1, 1 - par)

                first = 1
                for _ in steps_between:
                    body(first, (b + first) % 2)
                    first += 1
                for stop in sorted(between) + [n]:
                    assert first <= stop
                    tiles(dve, first, stop, lambda i, u: body(i, bank_of(b, first, u)))
                    if stop in between:
                        between[stop]()
                    first = stop
                if leave:
                    leave(n - 1, (b + n - 1) % 2)

            dve.wait_ge(pos_loaded, 16)
            dve.wait_ge(consts_loaded, 32)
            link(dve.tensor_copy(pos_f[:, 0, :], pos_i[:, 0, :].bitcast(I32)))
            for kind in range(3):
                ins = dve.tensor_scalar(rope_s[:, kind, :], pos_f[:, 0, :], c_freq[:, kind:kind + 1], None, ALU.mult)
            link(ins)
            reduce_angle(dve, link, rope_s, turns)
            link(dve.scalar_tensor_tensor(rope_c, rope_s, -1.0, rope_s, ALU.mult, ALU.max))
            dve.tensor_scalar(rope_c, rope_c, -1.0, math.pi / 2, ALU.mult, ALU.add).then_inc(angle_ready, 2)

            rms(0, x_t, 16, D, c_mix, x_t, tmp, begun="proj1")
            split_act(x_t, 0, norm=True)
            stage("proj1")

            dve.wait_ge(tile_out, evac["gates1"])
            dve.wait_ge(sin_ready, 1)
            cq, ckv = proj[:, CQ:CQ + 4], proj[:, CKV:CKV + 2]
            rms(1, cq, 4, Q_RANK, c_qn, cq, low_sq[:, 0:4])
            scaled(cq).then_inc(norm_ready, 1)
            rms(2, ckv, 2, KV_RANK, c_kvn, ckv, low_sq[:, 4:6])
            scaled(ckv).then_inc(norm_ready, 1)

            def rotated(j):
                x, kind = rots[j]
                bank = 2 + j if j < 6 else 6 + j % 2
                cos = rope_c[:, kind, :].unsqueeze(1).broadcast_to([P, 2, T])
                sin = rope_s[:, kind, :].unsqueeze(1).broadcast_to([P, 2, T])
                dve.wait_ge(rot_done, j + 1)
                if j >= 1:
                    dve.wait_ge(rot_used, j)
                if isinstance(x, int):
                    dst = (k_pe, ik)[x // 2][:, x % 2, :]
                    dve.tensor_tensor(rot_tmp[:, 0, :], psum[:, bank, T:2 * T], rope_s[:, kind, :], ALU.mult)
                    link(dve.tensor_tensor(dst, psum[:, bank, 0:T], rope_c[:, kind, :], ALU.mult))
                    dve.tensor_tensor(dst, dst, rot_tmp[:, 0, :], ALU.add).then_inc(rot_used, 1)
                else:
                    dve.tensor_tensor(rot_tmp, psum[:, bank, :].rearrange("p (a t) -> p a t", a=2), sin, ALU.mult)
                    link(dve.tensor_tensor(x, x, cos, ALU.mult))
                    dve.tensor_tensor(x, x, rot_tmp, ALU.add).then_inc(rot_used, 1)

            def index(batch):
                t, h0 = batch // 2, 8 * (batch % 2)
                nk = P * (t + 1)
                dve.wait_ge(relu_done, batch + 1)
                if batch == 0:
                    dve.wait_ge(turn_out, 2)
                for n in range(8):
                    h = h0 + n
                    ins = dve.scalar_tensor_tensor(select[:, t, 0:nk], relu[:, n * nk:n * nk + nk], iw_row[:, t, h:h + 1],
                                                   (select if h else mask)[:, t, 0:nk], ALU.mult, ALU.add)
                    if n < 7:
                        link(ins)
                ins.then_inc(dots_used, 1)
                dve.wait_ge(dots_used, batch + 1)

            def top_round(_):
                for t in range(QT):
                    ins = dve.max(small[:, 8 * t:8 * t + 8], select[:, t, 0:P * (t + 1)])
                link(ins)
                for t in range(QT):
                    nk = P * (t + 1)
                    ins = dve.match_replace(select[:, t, 0:nk], small[:, 8 * t:8 * t + 8], select[:, t, 0:nk], REPLACED)
                link(ins)

            def selection():
                for t in range(QT):
                    nk = P * (t + 1)
                    ins = dve.tensor_scalar(select[:, t, 0:nk], select[:, t, 0:nk], REPLACED / 2, NEG, ALU.is_gt, ALU.mult)
                link(ins)

            def shift(p):
                br = p // 8
                dve.wait_ge(s_done, p + 1)
                if p >= 3:
                    dve.wait_ge(pt_done, p - 2)
                scale = ((MLA_NOPE + MLA_ROPE) if br == 0 else HEAD) ** -0.5
                for t in range(QT):
                    at, nk = P * t, P * (t + 1)
                    ins = dve.scalar_tensor_tensor(s_sb[:, p % 3, at:at + nk], psum[:, 2 + p % 2, at:at + nk], scale,
                                                   (select if br else mask)[:, t, 0:nk], ALU.mult, ALU.add)
                link(ins)
                for t in range(QT):
                    at, nk = P * t, P * (t + 1)
                    ins = dve.tensor_reduce(soft_c[:, p % 2, 0, t:t + 1], s_sb[:, p % 3, at:at + nk], AX.X, ALU.max, negate=True)
                ins.then_inc(s_shifted, 1)

            def normalise(p):
                dve.wait_ge(p_exp, p + 1)
                link(dve.reciprocal(soft_c[:, p % 2, 2, :], soft_c[:, p % 2, 1, :]))
                for t in range(QT):
                    s = s_sb[:, p % 3, P * t:P * t + P * (t + 1)]
                    ins = dve.tensor_scalar(s, s, soft_c[:, p % 2, 2, t:t + 1], None, ALU.mult)
                ins.then_inc(p_ready, 1)

            def attend():
                dve.wait_ge(up_out, 24)
                for step in range(1, ATTENTION_STEPS):
                    for j in rots_of(step - 1):
                        rotated(j)
                    for p in in_step(step, 11, 16):
                        normalise(p)
                    for batch in in_step(step, 5, 4):
                        index(batch)
                    for _ in in_step(step, 17, 1):
                        selection()
                    for p in in_step(step, 10, 16):
                        shift(p)
                    for r in in_step(step, 9, TOPK // 8):
                        top_round(r)
                    yield

            stage("gates1", steps_between=attend(), begun=False)
            dve.wait_ge(o_ready, 16)
            split_act(o_heads, 4 * base["branch1"], begun="branch1")

            def merge(i, par):
                dve.wait_ge(quarter_used, (i + base["branch1"]) * 4 + 4)
                for br in range(2):
                    g = gates[br][:, i, :]
                    ins = dve.tensor_tensor(g, psum[:, par, br * T:br * T + T], g, ALU.mult)
                    if br == 0:
                        ins.then_inc(gated, 1)
                ins.then_inc(tile_out, 1)
                dve.wait_ge(tile_out, i + (evac["branch1"] + 1))
                dve.tensor_tensor(merged[:, i, :], gates[0][:, i, :], gates[1][:, i, :], ALU.add).then_inc(merged_ready, 1)

            dve.wait_ge(gates_ready, 2)
            stage("branch1", merge)
            dve.wait_ge(merged_ready, 16)
            split_act(merged, 4 * base["out1"], begun="out1")
            dve.memset(peer_keys1, 0.0).then_inc(keys_clear, 1)

            def residual(i, par):
                dve.wait_ge(quarter_used, (i + base["out1"]) * 4 + 4)
                dve.tensor_tensor(x1[:, i, :], psum[:, par, 0:T], x1[:, i, :], ALU.add).then_inc(tile_out, 1)

            dve.wait_ge(x_again, 16)
            stage("out1", residual)
            add_experts = dve_experts(dve, 1, link, rms, split_act, low, stage)
            rms(4, xb, 16, D, c_fin, xb, tmp, before=add_experts)

            def block_output(some):
                scaled(xb[:, some]).then_inc(block_in, 1)
                dve.wait_ge(block_in, some.stop // 4)

            rms(5, xb, 16, D, c_n1, xn, tmp, begun="z2", before=block_output)
            split_act(xn, 4 * base["z2"], norm=True)
            stage("z2", steps_between=dve_s5(dve, link))
            dve_glu(dve)
            dve_mlstm(dve, link)
            dve.wait_ge(glu_out, 8)
            dve.wait_ge(hmt_out, 8)
            split_act(mix, 4 * base["out2"], begun="out2")

            def residual2(i, par):
                dve.wait_ge(quarter_used, (i + base["out2"]) * 4 + 4)
                dve.tensor_tensor(x1[:, i, :], psum[:, par, 0:T], x1[:, i, :], ALU.add).then_inc(tile_out, 1)

            dve.wait_ge(x_again, 48)
            stage("out2", residual2)
            add_experts = dve_experts(dve, 2, link, rms, split_act, low, stage)
            rms(7, xb, 16, D, c_fin2, xb, tmp, before=add_experts)
            for c in range(4):
                scaled(xb[:, 4 * c:4 * c + 4]).then_inc(block_in, 1)



TWO_PI = [6.28125, 0.0019340515136718750, 1.2556659146e-6]


def reduce_angle(dve, link, angle, turns):
    magic = 12582912.0
    link(dve.tensor_scalar(turns, angle, 1 / (2 * math.pi), magic, ALU.mult, ALU.add))
    link(dve.tensor_scalar(turns, turns, magic, None, ALU.subtract))
    for part in TWO_PI:
        link(dve.scalar_tensor_tensor(angle, turns, -part, angle, ALU.mult, ALU.add))
    link(dve.tensor_scalar(angle, angle, 3.1415925, -3.1415925, ALU.min, ALU.max))


def weight_tiles(w):
    m = w.shape[1] // P
    return np.ascontiguousarray(w.reshape(2, 8, P, m, P).transpose(3, 0, 2, 1, 4).reshape(m, 2, P, 1024))


def by_rows(w, k):
    return np.ascontiguousarray(w.reshape(k, P, -1).transpose(1, 0, 2))


def lay_out(i):
    x = {k: np.asarray(v) for k, v in i.items()}
    col = lambda v: v.reshape(-1, P).T
    mats, freq, mask = rope_and_masks()
    w = x["w_in"][0]
    cut = lambda lo, hi: w[:, lo:hi]
    uq = x["mla_w_uq"][0]
    z = x["w_in_2"][0]
    bias = np.zeros((P, 1), np.float32)
    bias[0:8, 0] = x["b_gates_2"][0]
    pair = (np.arange(P)[:, None] // 64 == np.arange(2)[None, :]).astype(np.float32)
    eight = (np.arange(P)[:, None] // 16 == np.arange(8)[None, :]).astype(np.float32)
    s = np.arange(P)
    tri = np.concatenate([s[:, None] <= s[None, :], np.where(s[None, :] <= s[:, None], 0.0, NEG)], 1).astype(np.float32)

    def states(v):
        return np.ascontiguousarray(v.reshape(S5_TILES, P, -1).transpose(1, 0, 2).reshape(P, S5_TILES, -1).squeeze()
                                    if v.size == S5_TILES * P else v.reshape(S5_TILES, P, -1).transpose(1, 0, 2))

    first = np.concatenate([cut(0, 768), cut(768, 832), cut(3392, 3456), cut(832, 3392), cut(3456, 3584)], 1)
    d = {
        "x": by_rows(x["x"][0].T, KT),
        "positions": x["positions"].reshape(T),
        "cols": np.ascontiguousarray(np.concatenate([col(x["norm_mix_g"]), col(x["mla_q_norm_g"]), col(x["mla_kv_norm_g"]),
                                col(x["norm_ffn_g"]), col(x["norm_final_g"]), freq,
                                col(x["norm1_g_2"]), col(x["mlstm_norm_g_2"]), col(x["norm2_g_2"]), col(x["final_g_2"]),
                                bias, np.full((P, 1), math.pi / 2, np.float32), pair, eight, col(x["s5_d_2"]),
                                x["conv_qk_w_2"][0].reshape(4, KT, P).transpose(2, 1, 0).reshape(P, -1)], 1)),
        "consts": np.ascontiguousarray(np.stack([np.eye(P), np.tile(np.arange(P), (P, 1)), np.ones((P, P))], 1).astype(np.float32)),
        "mats": mats, "mask": mask,
        "w_proj1": weight_tiles(first),
        "w_gates1": weight_tiles(cut(3472, 7568)),
        "w_uq": by_rows(np.concatenate([uq[..., :MLA_NOPE].reshape(Q_RANK, -1), uq[..., MLA_NOPE:].reshape(Q_RANK, -1)], 1), 4), "w_uk": by_rows(x["mla_w_uk"][0], 2), "w_uv": by_rows(x["mla_w_uv"][0], 2),
        "w_branch1": weight_tiles(np.concatenate([x["w_branch_a"][0], x["w_branch_b"][0]], 0)),
        "w_out1": weight_tiles(x["w_out"][0]),
        "w_q1": weight_tiles(x["peer_w_q"][0].reshape(D, -1)),
        "keys1": np.ascontiguousarray(x["peer_sub_keys"][0].transpose(1, 3, 0, 2).reshape(P, PEER_HEADS, NKEYS)),
        "tri": tri,
        "lam": np.ascontiguousarray(np.stack([states(x["s5_lambda_re_2"]), states(x["s5_lambda_im_2"]),
                                              states(np.repeat(x["s5_log_dt_2"][0][:, None], S5_STATE, 1))], 1)),
        "b_re": states(x["s5_b_re_2"]), "b_im": states(x["s5_b_im_2"]),
        "c_re": states(x["s5_c_re_2"][0].transpose(0, 2, 1)), "c_im": states(x["s5_c_im_2"][0].transpose(0, 2, 1)),
        "glu": np.ascontiguousarray(x["s5_glu_w_2"].reshape(8, P, 32).transpose(1, 0, 2)),
        "w_z2": weight_tiles(np.concatenate([z[:, 4104:], z[:, 4096:4224], z[:, :4096]], 1)),
        "w_out2": weight_tiles(x["w_out_2"][0]), "w_q2": weight_tiles(x["peer_wq_2"][0]),
        "keys2": np.ascontiguousarray(x["peer_subkeys_2"][0].transpose(2, 0, 1)),
        "u2": expert_rows(x["peer_u_2"][0]), "v2": expert_columns(x["peer_v_2"][0]),
        "u1": expert_rows(x["peer_u"][0]), "v1": expert_columns(x["peer_v"][0]),
    }
    return d


def expert_rows(u):
    return np.ascontiguousarray(u.reshape(NKEYS, NKEYS, 2, 8, P).transpose(1, 2, 4, 3, 0).reshape(NKEYS, 2, P, 1024))


def expert_columns(v):
    return np.ascontiguousarray(v.reshape(NKEYS, NKEYS, 2, 1024).transpose(1, 2, 0, 3))


def kernel(**inputs):
    import concourse.bacc as bacc
    from concourse.bass_utils import run_bass_kernel_spmd

    nc = bacc.Bacc("TRN2", target_bir_lowering=False, num_devices=1)
    arrays = lay_out(inputs)
    aps = {name: nc.dram_tensor("in_" + name, v.shape, mybir.dt.from_np(v.dtype), kind="ExternalInput").ap()
           for name, v in arrays.items()}
    aps["out"] = nc.dram_tensor("out_rows", (P, KT, T), F32, kind="ExternalOutput").ap()
    build_two_blocks(nc, aps)
    r = run_bass_kernel_spmd(nc, [{"in_" + name: v for name, v in arrays.items()}], core_ids=[0])
    out = r.results[0]["out_rows"]
    return np.ascontiguousarray(out.transpose(1, 0, 2).reshape(D, T).T).reshape(1, T, D)
```
